# Optimizing a Trainium2 kernel written in Bass

```python
import math
import jax, jax.numpy as jnp
from jax import lax
import numpy as np

D_MODEL = 1024
BATCH = 1
SEQ = 128
DEPTH = 2
DEC_BATCH = 1
DEC_SEQ = 512
PAST_LEN = 128

GRID_W = 64
N_HEADS = 8
QK_NOPE = 64
QK_ROPE = 32
V_DIM = 64
Q_RANK = 384
KV_RANK = 256
ROPE_BASE = 10000.0
Q_BLOCK = 128
HY_WIDTH = 512
HY_ORDER = 2
HY_BANDS = 16
HY_EMB = 1 + 2 * HY_BANDS
HY_HIDDEN = 64
SHORT_K = 3
P_HEADS = 8
N_KEYS = 128
N_EXPERTS = N_KEYS * N_KEYS
KEY_DIM = 256
KEY_HALF = KEY_DIM // 2
P_TOPK = 16
TOK_BLOCK = 128
IN_COLS = Q_RANK + KV_RANK + QK_ROPE + (HY_ORDER + 1) * HY_WIDTH + 2 * D_MODEL
EPS = 1e-6

kernel_name = 'hybrid_mla_hyena_peer_diffusion_step'

def _rmsnorm(x, g):
    xf = x.astype(jnp.float32)
    y = xf * lax.rsqrt(jnp.mean(xf * xf, axis=-1, keepdims=True) + EPS)
    return (y * g.astype(jnp.float32)).astype(x.dtype)

def _adaln(cvec, w, b):
    m = jax.nn.silu(cvec) @ w + b
    return jnp.split(m[..., None, :], 6, axis=-1)

def _axial_rope(n_tok):
    rows = n_tok // GRID_W
    row = jnp.repeat(jnp.arange(rows, dtype=jnp.float32), GRID_W)
    col = jnp.tile(jnp.arange(GRID_W, dtype=jnp.float32), rows)
    n_freq = QK_ROPE // 4
    inv = 1.0 / (ROPE_BASE ** (jnp.arange(n_freq, dtype=jnp.float32) / n_freq))
    ang = jnp.concatenate([row[:, None] * inv, col[:, None] * inv], axis=-1)
    return jnp.cos(ang), jnp.sin(ang)

def _apply_rope(x, cos, sin):
    half = QK_ROPE // 2
    x1 = x[..., :half].astype(jnp.float32)
    x2 = x[..., half:].astype(jnp.float32)
    return jnp.concatenate([x1 * cos - x2 * sin, x2 * cos + x1 * sin], axis=-1).astype(x.dtype)

def _mla_attend(qn, qr, kn, kr, v):
    B, Lq = qn.shape[0], qn.shape[1]
    nb = Lq // Q_BLOCK
    scale = 1.0 / math.sqrt(QK_NOPE + QK_ROPE)
    qn_b = qn.reshape(B, nb, Q_BLOCK, N_HEADS, QK_NOPE).swapaxes(0, 1)
    qr_b = qr.reshape(B, nb, Q_BLOCK, N_HEADS, QK_ROPE).swapaxes(0, 1)

    def block(args):
        qn_i, qr_i = args
        s = jnp.einsum('bqhd,bkhd->bhqk', qn_i, kn) + jnp.einsum('bqhr,bkr->bhqk', qr_i, kr)
        p = jax.nn.softmax(s.astype(jnp.float32) * scale, axis=-1).astype(v.dtype)
        return jnp.einsum('bhqk,bkhd->bqhd', p, v)

    o = lax.map(block, (qn_b, qr_b))
    return o.swapaxes(0, 1).reshape(B, Lq, N_HEADS * V_DIM)

def _hyena_filters(n_tok, w1, b1, w2, b2, w3, decay):
    f32 = jnp.float32
    t = jnp.arange(n_tok, dtype=f32) / n_tok
    bands = jnp.arange(1, HY_BANDS + 1, dtype=f32)
    ang = 2.0 * math.pi * t[:, None] * bands
    z = jnp.concatenate([t[:, None], jnp.sin(ang), jnp.cos(ang)], axis=-1)
    f = jnp.sin(z @ w1.astype(f32) + b1.astype(f32))
    f = jnp.sin(f @ w2.astype(f32) + b2.astype(f32))
    h = (f @ w3.astype(f32)).reshape(n_tok, HY_ORDER, 2, HY_WIDTH)
    window = jnp.exp(-decay.astype(f32)[None] * t[:, None, None, None])
    return h * window

def _fft_conv(u, h):
    n = u.shape[1]
    uf = jnp.fft.rfft(u, n=2 * n, axis=1)
    hf = jnp.fft.rfft(h, n=2 * n, axis=0)
    return jnp.fft.irfft(uf * hf[None], n=2 * n, axis=1)[:, :n]

def _bidir_long_conv(u, h_fwd, h_bwd, bias):
    fwd = _fft_conv(u, h_fwd)
    bwd = jnp.flip(_fft_conv(jnp.flip(u, axis=1), h_bwd), axis=1)
    return fwd + bwd + u * bias

def _short_conv(x, w, b):
    n = x.shape[1]
    pad = SHORT_K // 2
    xp = jnp.pad(x, ((0, 0), (pad, pad), (0, 0)))
    y = xp[:, 0:n] * w[0]
    for k in range(1, SHORT_K):
        y = y + xp[:, k:k + n] * w[k]
    return y + b

def _hyena(z, conv_w, conv_b, filt, bias):
    z = _short_conv(z, conv_w, conv_b).astype(jnp.float32)
    parts = jnp.split(z, HY_ORDER + 1, axis=-1)
    y = parts[0]
    for o in range(HY_ORDER):
        y = parts[o + 1] * _bidir_long_conv(y, filt[:, o, 0], filt[:, o, 1], bias[o].astype(jnp.float32))
    return y

def _peer(h, wq, sub_keys, u_tab, v_tab):
    B, L, D = h.shape
    T = B * L
    xt = h.reshape(T, D)
    q = (xt @ wq).reshape(T, P_HEADS, 2, KEY_HALF)
    s = jnp.einsum('thpk,hpnk->thpn', q, sub_keys).astype(jnp.float32)
    s1, i1 = lax.top_k(s[:, :, 0], P_TOPK)
    s2, i2 = lax.top_k(s[:, :, 1], P_TOPK)
    cand = (s1[..., :, None] + s2[..., None, :]).reshape(T, P_HEADS, P_TOPK * P_TOPK)
    cidx = (i1[..., :, None] * N_KEYS + i2[..., None, :]).reshape(T, P_HEADS, P_TOPK * P_TOPK)
    top, pos = lax.top_k(cand, P_TOPK)
    idx = jnp.take_along_axis(cidx, pos, axis=-1)
    g = jax.nn.softmax(top, axis=-1).astype(h.dtype)
    nb = T // TOK_BLOCK
    xb = xt.reshape(nb, TOK_BLOCK, D)
    ib = idx.reshape(nb, TOK_BLOCK, P_HEADS, P_TOPK)
    gb = g.reshape(nb, TOK_BLOCK, P_HEADS, P_TOPK)

    def block(args):
        x_i, i_i, g_i = args
        u = jnp.take(u_tab, i_i, axis=0)
        a = jax.nn.gelu(jnp.einsum('td,thkd->thk', x_i, u))
        return jnp.einsum('thk,thkd->td', a * g_i, jnp.take(v_tab, i_i, axis=0))

    out = lax.map(block, (xb, ib, gb))
    return out.reshape(B, L, D)

def _layer(x, mod, lp, rope, ctx):
    shift1, scale1, gate1, shift2, scale2, gate2 = mod
    B, L, _ = x.shape
    h = _rmsnorm(x, lp['norm_mix']) * (1 + scale1) + shift1
    proj = h @ lp['w_in']
    cuts = [Q_RANK, Q_RANK + KV_RANK, Q_RANK + KV_RANK + QK_ROPE,
            Q_RANK + KV_RANK + QK_ROPE + (HY_ORDER + 1) * HY_WIDTH]
    cq, ckv, kr, hy_in, gates = jnp.split(proj, cuts, axis=-1)
    ckv = _rmsnorm(ckv, lp['kv_norm'])
    q = (_rmsnorm(cq, lp['q_norm']) @ lp['w_uq']).reshape(B, L, N_HEADS, QK_NOPE + QK_ROPE)
    qn, qr = q[..., :QK_NOPE], q[..., QK_NOPE:]
    kr_keys = kr
    if rope is not None:
        cos, sin = rope
        qr = _apply_rope(qr, cos[:, None], sin[:, None])
        kr_keys = _apply_rope(kr, cos, sin)
    ckv_keys = ckv
    if ctx is not None:
        ctx_ckv, ctx_kr = ctx
        ckv_keys = jnp.concatenate([ctx_ckv, ckv], axis=1)
        kr_keys = jnp.concatenate([ctx_kr, kr_keys], axis=1)
    kv = (ckv_keys @ lp['w_ukv']).reshape(B, -1, N_HEADS, QK_NOPE + V_DIM)
    attn = _mla_attend(qn, qr, kv[..., :QK_NOPE], kr_keys, kv[..., QK_NOPE:])
    filt = _hyena_filters(L, lp['hy_w1'], lp['hy_b1'], lp['hy_w2'], lp['hy_b2'], lp['hy_w3'], lp['hy_decay'])
    hy = _hyena(hy_in, lp['hy_conv_w'], lp['hy_conv_b'], filt, lp['hy_bias']).astype(x.dtype)
    g_a, g_b = jnp.split(jax.nn.sigmoid(gates), 2, axis=-1)
    merged = g_a * (attn @ lp['w_oa']) + g_b * (hy @ lp['w_ob'])
    x = x + gate1 * (merged @ lp['w_out'])
    h2 = _rmsnorm(x, lp['norm_ffn']) * (1 + scale2) + shift2
    x = x + gate2 * _peer(h2, lp['peer_wq'], lp['peer_keys'], lp['peer_u'], lp['peer_v'])
    return x, ckv, kr

def setup_inputs(seed: int = 0) -> dict:
    key = jax.random.key(seed)
    ks = iter(jax.random.split(key, 40))

    def nrm(shape, s):
        return jax.random.normal(next(ks), shape, jnp.float32) * s

    D = D_MODEL
    return {
        'x_prompt': nrm((BATCH, SEQ, D), 1.0),
        'x_sample': nrm((DEC_BATCH, DEC_SEQ, D), 1.0),
        'cache_ckv': nrm((DEC_BATCH, DEPTH, PAST_LEN, KV_RANK), 1.0),
        'cache_krope': nrm((DEC_BATCH, DEPTH, PAST_LEN, QK_ROPE), 1.0),
        'c': nrm((DEC_BATCH, D), 1.0),
        'c_ctx': nrm((D,), 1.0),
        'w_ada': nrm((DEPTH, D, 6 * D), 0.5 * D ** -0.5),
        'b_ada': nrm((DEPTH, 6 * D), 0.01),
        'norm_mix': 1.0 + nrm((DEPTH, D), 0.02),
        'norm_ffn': 1.0 + nrm((DEPTH, D), 0.02),
        'w_in': nrm((DEPTH, D, IN_COLS), D ** -0.5),
        'q_norm': 1.0 + nrm((DEPTH, Q_RANK), 0.02),
        'kv_norm': 1.0 + nrm((DEPTH, KV_RANK), 0.02),
        'w_uq': nrm((DEPTH, Q_RANK, N_HEADS * (QK_NOPE + QK_ROPE)), Q_RANK ** -0.5),
        'w_ukv': nrm((DEPTH, KV_RANK, N_HEADS * (QK_NOPE + V_DIM)), KV_RANK ** -0.5),
        'w_oa': nrm((DEPTH, N_HEADS * V_DIM, D), (N_HEADS * V_DIM) ** -0.5),
        'w_ob': nrm((DEPTH, HY_WIDTH, D), HY_WIDTH ** -0.5),
        'w_out': nrm((DEPTH, D, D), D ** -0.5),
        'hy_conv_w': nrm((DEPTH, SHORT_K, (HY_ORDER + 1) * HY_WIDTH), SHORT_K ** -0.5),
        'hy_conv_b': nrm((DEPTH, (HY_ORDER + 1) * HY_WIDTH), 0.01),
        'hy_w1': nrm((DEPTH, HY_EMB, HY_HIDDEN), HY_EMB ** -0.5),
        'hy_b1': nrm((DEPTH, HY_HIDDEN), 0.1),
        'hy_w2': nrm((DEPTH, HY_HIDDEN, HY_HIDDEN), HY_HIDDEN ** -0.5),
        'hy_b2': nrm((DEPTH, HY_HIDDEN), 0.1),
        'hy_w3': nrm((DEPTH, HY_HIDDEN, HY_ORDER * 2 * HY_WIDTH), 0.1 * HY_HIDDEN ** -0.5),
        'hy_decay': jax.random.uniform(next(ks), (DEPTH, HY_ORDER, 2, HY_WIDTH), jnp.float32, 1.0, 10.0),
        'hy_bias': nrm((DEPTH, HY_ORDER, HY_WIDTH), 0.1),
        'peer_wq': nrm((DEPTH, D, P_HEADS * KEY_DIM), D ** -0.5),
        'peer_keys': nrm((DEPTH, P_HEADS, 2, N_KEYS, KEY_HALF), KEY_HALF ** -0.5),
        'peer_u': nrm((DEPTH, N_EXPERTS, D), D ** -0.5),
        'peer_v': nrm((DEPTH, N_EXPERTS, D), P_HEADS ** -0.5),
        'final_norm': 1.0 + nrm((D,), 0.02),
    }

def reference(x_prompt, x_sample, cache_ckv, cache_krope, c, c_ctx, w_ada, b_ada, norm_mix, norm_ffn,
              w_in, q_norm, kv_norm, w_uq, w_ukv, w_oa, w_ob, w_out, hy_conv_w, hy_conv_b,
              hy_w1, hy_b1, hy_w2, hy_b2, hy_w3, hy_decay, hy_bias,
              peer_wq, peer_keys, peer_u, peer_v, final_norm):
    rope = _axial_rope(x_sample.shape[1])
    xp, xs = x_prompt, x_sample
    new_ckv, new_kr = [], []
    for l in range(DEPTH):
        lp = {
            'norm_mix': norm_mix[l], 'norm_ffn': norm_ffn[l], 'w_in': w_in[l],
            'q_norm': q_norm[l], 'kv_norm': kv_norm[l], 'w_uq': w_uq[l], 'w_ukv': w_ukv[l],
            'w_oa': w_oa[l], 'w_ob': w_ob[l], 'w_out': w_out[l],
            'hy_conv_w': hy_conv_w[l], 'hy_conv_b': hy_conv_b[l],
            'hy_w1': hy_w1[l], 'hy_b1': hy_b1[l], 'hy_w2': hy_w2[l], 'hy_b2': hy_b2[l], 'hy_w3': hy_w3[l],
            'hy_decay': hy_decay[l], 'hy_bias': hy_bias[l],
            'peer_wq': peer_wq[l], 'peer_keys': peer_keys[l], 'peer_u': peer_u[l], 'peer_v': peer_v[l],
        }
        mod_ctx = _adaln(c_ctx, w_ada[l], b_ada[l])
        xp, ckv_p, kr_p = _layer(xp, mod_ctx, lp, None, None)
        new_ckv.append(ckv_p)
        new_kr.append(kr_p)
        mod_lat = _adaln(c, w_ada[l], b_ada[l])
        xs, _, _ = _layer(xs, mod_lat, lp, rope, (cache_ckv[:, l], cache_krope[:, l]))
    y_prompt = _rmsnorm(xp, final_norm)
    y_sample = _rmsnorm(xs, final_norm)
    state_ckv = jnp.stack(new_ckv, axis=1)
    state_krope = jnp.stack(new_kr, axis=1)
    return (y_prompt, y_sample, state_ckv, state_krope)


_drawn_inputs = setup_inputs


def setup_inputs(seed=0):
    import zlib

    import numpy as np

    out = dict(_drawn_inputs(seed))
    spreads = {}
    factors = {'cache_ckv': 5.988,
     'cache_krope': 8.0,
     'b_ada': 3.922,
     'norm_mix': 2.967,
     'norm_ffn': 4.453,
     'q_norm': 8.0,
     'kv_norm': 2.831,
     'hy_conv_b': 6.536,
     'final_norm': 2.899}
    for name, (base, spread) in spreads.items():
        noise = np.random.default_rng([zlib.crc32(name.encode()), seed]).standard_normal(out[name].shape)
        drawn = base * np.exp(spread * noise) if base else spread * noise
        out[name] = __import__('jax').numpy.asarray(drawn.astype(out[name].dtype))
    for name, factor in factors.items():
        out[name] = (out[name] * factor).astype(out[name].dtype)
    return out
```

```python
import math
from contextlib import ExitStack

import concourse.bass as bass
import numpy as np
from concourse import mybir

D, KD = 1024, 8
DEPTH, SEQ, DEC_SEQ, PAST, GRID_W = 2, 128, 512, 128, 64
NH, NOPE, ROPE, VD, QR, KVR = 8, 64, 32, 64, 384, 256
HQ = NOPE + ROPE
HYW, HID, EMB, BANDS = 512, 64, 33, 16
PH, NK, TOPK = 8, 128, 16
NHP = 2 * PH
N_EXPERTS = NK * NK
IN_COLS = QR + KVR + ROPE + 3 * HYW + 2 * D
HY0, GT0 = QR + KVR + ROPE, QR + KVR + ROPE + 3 * HYW
EPS = 1e-6
TILES = (SEQ + DEC_SEQ) // 128
SLOTS = PH * TOPK
NB = 8
HALF = NB // 2
ITERS = SLOTS // NB
WIDTHS = [TOPK // (i + 1) for i in range(TOPK)]
NC = sum(WIDTHS)
RUNS = [(0, 1, 16), (1, 1, 8), (2, 1, 5), (3, 1, 4), (4, 1, 3), (5, 3, 2), (8, 8, 1)]
MAGIC = 12582912.0
TWO_PI_HI = 6.28125
TWO_PI_LO = 2.0 * math.pi - TWO_PI_HI
GELU_A, GELU_C = 0.044715, math.sqrt(2.0 / math.pi)
SLOT_W = 2048


class Group:

    def __init__(self, name):
        self.name, self.latent = name, name == "s"
        self.t0, self.nt, self.nk, self.gi = (1, 4, 5, 1) if self.latent else (0, 1, 1, 0)
        self.T, self.TK = self.nt * 128, self.nk * 128
        self.ckv_banks = -(-2 * self.nk // 4)
        self.kr_banks = -(-self.nk // 4)
        self.k_pieces = ([(h, 1, 0, 4) for h in range(NH)] if self.latent else []) + \
            [(h, 4, self.nk - 1, 1) for h in (0, 4)]
        self.s = {}


def weight_loads(groups):
    loads = [(("ada", i), 1, (None, "ada_ps", i + 1)) for i in range(24)]
    for g in groups:
        n = g.name
        loads.append(((n, "qkv"), 3, (n, "qkv_ps", 2 * g.nt)))
        loads.append(((n, "ukv"), 1, (n, "v_ps", g.nk)))
        loads.append(((n, "uq"), 2, (n, "q_ps", g.nt)))
        loads += [((n, "hy", i), 1, (n, "hyc_ps", 2 * i + 2)) for i in range(6)]
        loads += [((n, "C"), 1, (n, "K_ps", 4 * g.nt)), ((n, "S"), 1, (n, "K_ps", 4 * g.nt)),
                  ((n, "Mc"), 1, (n, "y_ps", 8)), ((n, "Ms"), 1, (n, "y_ps", 8))]
        for i in range(4):
            c = 4 * 2 * (i + 1)
            loads += [((n, "ga", i), 1, (n, "mg_ps", c)), ((n, "gb", i), 1, (n, "mg_ps", c)),
                      ((n, "oab", i), 1, (n, "mg_ps", c))]
        loads += [((n, "out", i), 1, (n, "out_ps", (i + 1) * g.nt)) for i in range(4)]
        loads += [((n, "keys"), 1, (n, "sc_ps", NHP))]
        loads += [((n, "wq", i), 1, (n, "qh_ps", 2 * i + 2)) for i in range(8)]
    placed, at, held = {}, 0, None
    for name, k, free in loads:
        if name[-1] == "keys":
            placed[name] = (3, 1, free)
            at, held = 0, 3
            continue
        if held is not None and name[1] != "wq":
            at, held = 0, None
        ring = 3 if held is not None else 4
        if at + k > ring:
            at = 0
        placed[name] = (at, k, free)
        at = (at + k) % ring
    return placed


GROUP_SEMS = """ss1 xn tr1 hT1 qkv_ps qkv_raw ss_qkv cn trc cT q_ps q_tm q_rope trq qT k_ps kT v_ps v
 s_ps smax prob trp pT o_ps attn tra aT hyc_ps hyc_mid hyc f_ps f_red f h_ps win wh sd K_ps K
 tru u U_ps Ym Yc y_ps y mg_ps th mm mg dgr bias0 row_ps row out_ps r2 xadd ss2 h2 tr2 hT2
 qh_ps qh sc_ps sc top ge gw ctx state arrived""".split()
SHARED_SEMS = """ada_ps mod chain pchain slot0 slot1 slot2 slot3 lvec lrow lfil ldec0 ldec1 lw3a lw3b
 buf_free staged turn ttr p_small inner th_e w_ready diag acc_read h2c""".split()


def build(nc, I, O):
    f32, u32, i32 = mybir.dt.float32, mybir.dt.uint32, mybir.dt.int32
    ALU, ACT, AX = mybir.AluOpType, mybir.ActivationFunctionType, mybir.AxisListType
    GR = [Group("p"), Group("s")]
    LOADS = weight_loads(GR)
    ctx = ExitStack()
    with ctx:
        def sb(name, words, dt=f32, parts=128):
            return ctx.enter_context(nc.sbuf_tensor("sb_" + name, [parts, words], dt))

        xflat = sb("x", TILES * D)
        x = xflat[:, :].rearrange("p (t d) -> p t d", d=D)
        hT = sb("hT", KD * 512)
        g2 = sb("g2", 2 * D)[:, :].rearrange("p (g d) -> p g d", g=2)
        slots = sb("slots", 4 * SLOT_W)
        keep = sb("keep", 4096)
        h2p = sb("h2p", D)
        arena = sb("arena", 22400)
        idx = sb("idx", TILES * SLOTS, u32)
        gwt = sb("gwt", TILES * SLOTS)
        ident, ones, zeros = sb("ident", 128), sb("ones", 128), sb("zeros", 128)
        cfm, cth = sb("cfm", 16), sb("cth", 16)
        mod = sb("mod", 96)[:, :].rearrange("p (c g) -> p c g", g=2)
        fold = sb("fold", 48)[:, :].rearrange("p (v c g) -> p v c g", v=3, g=2)
        lvec = sb("lvec", 64)
        qn_row, kvn_row = sb("qn_row", QR), sb("kvn_row", KVR)
        krp = sb("krp", 5 * HQ)[:, :].rearrange("p (k c) -> p k c", c=HQ)
        trig = sb("trig", 2 * 4 * ROPE)[:, :].rearrange("p (v j c) -> p v j c", v=2, j=4)
        negt = sb("negt", TILES)
        loff = sb("loff", 1)
        convw = sb("convw", 48)[:, :].rearrange("p (m v) -> p m v", v=4)
        fw1, fw2, fb = sb("fw1", HID, parts=EMB), sb("fw2", HID, parts=HID), sb("fb", 2, parts=HID)
        zT = sb("zT", SEQ + DEC_SEQ, parts=EMB)
        hyb = sb("hyb", 2 * HYW, parts=1)
        iota = sb("iota", NC)
        st = sb("st", 64)
        ssum = sb("ssum", 64)
        nmax = sb("nmax", 4)

        ps = ctx.enter_context(nc.psum_tensor("ps", [128, 8, 512], f32))
        psf = ps[:, :, :].rearrange("p b n -> p (b n)")

        def sem(name):
            return ctx.enter_context(nc.semaphore("k_" + name))

        setup, silu, out_done, final, fch, go = (sem(n) for n in ("setup", "silu", "out_done", "final", "fch", "go"))
        passed, final_sq = sem("passed"), sem("final_sq")
        Z = {n: sem(n) for n in SHARED_SEMS}
        nums = [v.num for v in Z.values()]
        gath = [sem(f"gath{b}") for b in range(NB)]
        of_group = {n: sem("g_" + n) for n in GROUP_SEMS}
        GR[0].s = GR[1].s = of_group
        group_nums = [v.num for v in of_group.values()]
        for part in (nums, group_nums):
            assert part == list(range(part[0], part[0] + len(part)))
        slot_full = [Z["slot0"], Z["slot1"], Z["slot2"], Z["slot3"]]

        def a(at, words):
            return arena[:, at:at + words]

        def a3(at, n, m):
            return arena[:, at:at + n * m].rearrange("p (n m) -> p n m", m=m)

        xn = a3(0, 4, D)
        xn2 = a3(8192, 4, D)
        cqraw, kvraw, cqn = a3(0, 4, QR), a3(1536, 4, 288), a3(2688, 4, QR)
        prob, probT, attn_all = a3(0, 2, 640), a3(1280, 2, 640), a3(2560, 4, 512)
        ckvn = a3(4224, 5, KVR)
        cqnT, ckvT = a3(5504, 3, 512), a(7040, 1280)
        q_tm = a3(8320, 2, 768)
        rope_tmp = a(9856, 768)
        qT, KT, V = a3(10624, 8, 512), a(14720, 5120), a3(19840, 5, 512)
        junk = a(21376, 1024)
        hyT = a3(0, 12, 512)
        Kf = a(6144, 4096).rearrange("p (r k n) -> p r k n", r=2, k=4)
        Yf = a(10240, 4096).rearrange("p (r k n) -> p r k n", r=2, k=4)
        u_tm = a3(14336, 4, 512)
        w3 = arena[0:HID, 14336:14336 + 2048]
        decay = a3(16384, 2, 512)
        win, wh = a3(17408, 2, 512), a3(18432, 4, 512)
        prodm = a(17408, 4096).rearrange("p (b v n) -> p b v n", b=2, v=4)
        ftmp = a3(20480, 3, 512)
        f1T, f2T = arena[0:HID, 6144:6656], arena[0:HID, 21504:22016]
        mergedT = a3(0, 8, 512)
        tg, mtmp = a3(4096, 4, 512), a3(6144, 4, 512)
        rows = a3(12288, 3, D)
        dgr = a3(15360, 8, 128)
        otmp = a3(16384, 2, 256)
        scores = a(0, 8192).rearrange("p (j h n) -> p j h n", j=4, h=NHP)
        scr = a3(8192, NHP, NK)
        s16, i16, i16f = a3(10240, NHP, 16), a3(10496, NHP, 16), a3(10752, NHP, 16)
        cand, cidx, scr2 = a3(11008, PH, NC), a3(11408, PH, NC), a3(11808, PH, NC)
        qh = a3(12288, 4, 512)
        eq = a(14336, 6400).rearrange("p (h k c) -> p h k c", h=PH, k=16)
        top, pos, posf = a3(20736, PH, 16), a3(20864, PH, 16), a3(20992, PH, 16)
        gex, gsum = a3(21120, PH, 16), a(21248, 8)
        gbuf = a3(0, NB, 2 * D)
        h2c, eacc = a(16384, D), a(18432, D)
        dge = a3(19456, NB, 128)
        dots, dsq, din, dth, dw = (a(20480 + 16 * i, 8) for i in range(5))
        estage = a(20600, NB).bitcast(u32)
        attnT, hyoT = (keep[:, i * 2048:(i + 1) * 2048].rearrange("p (c t) -> p c t", t=512) for i in (0, 1))
        h2s = keep[:, :].rearrange("p (j d) -> p j d", d=D)
        hT3 = hT[:, :].rearrange("p (k t) -> p k t", t=512)

        def slot_of(name, words=SLOT_W):
            s0, k, _ = LOADS[name]
            return slots[:, s0 * SLOT_W:s0 * SLOT_W + words]

        def h2_of(g, j):
            return h2s[:, j, :] if g.latent else h2p[:, :]

        def KTv(g):
            return KT[:, 0:NH * g.TK].rearrange("p (h t) -> p h t", h=NH)

        def signal(gname, s):
            if gname is None:
                return Z[s]
            return of_group[s]

        block = ctx.enter_context(nc.Block())

        def meet(eng, count):
            eng.drain().then_inc(of_group["arrived"], 1)
            eng.wait_ge(go, count)
            eng.sem_inc(passed)

        @block.sync
        def _(sp):
            sp.dma_start(x, I["x"].rearrange("(t p) d -> p t d", p=128)).then_inc(setup, 16)
            for dst, src in ((cfm, I["cond"]), (trig.rearrange("p v j c -> p (v j c)"), I["trig"]), (negt, I["negt"]),
                             (zT, I["zT"]), (ident, I["ident"]), (iota, I["iota"])):
                sp.dma_start(dst[:, :], src).then_inc(setup, 16)

            def source(name, l):
                kind = name[1] if name[0] in ("p", "s") else name[0]
                g = GR[1 if name[0] == "s" else 0]

                packed = {"ada": 256, "hy": 256, "ga": 256, "gb": 256, "oab": 256, "out": 256, "wq": 256, "qkv": HY0, "ukv": 1024, "uq": 768}
                if kind in packed:
                    w, m = I["w_" + kind], packed[kind]
                    n = w.shape[-1] // m
                    i = name[-1] if kind not in ("qkv", "ukv", "uq") else 0
                    return w[bass.ds(l, 1), i].rearrange("o p (n m) -> p (o n) m", m=m), (n, m)
                if kind == "keys":
                    return I["keysT"][bass.ds(l, 1)].rearrange("o p (h n) -> p (o h) n", h=NHP), (NHP, NK)
                src = {"C": 0, "S": 1, "Mc": 2, "Ms": 3}[kind]
                if g.latent:
                    return I["dft_s"][src], (4, 512)
                return I["dft_p"][src], (1, 128)

            with sp.Fori(0, DEPTH) as l:
                sp.dma_start(lvec[:, :], I["lvec"][bass.ds(l, 1)].rearrange("o p n -> p (o n)")).then_inc(Z["lvec"], 16)
                for dst, src in ((qn_row, I["q_norm"]), (kvn_row, I["kv_norm"])):
                    sp.dma_start(dst[:, :], src[bass.ds(l, 1), :].rearrange("o n -> (o n)").partition_broadcast(128)).then_inc(Z["lrow"], 16)
                sp.dma_start(loff[:, :], I["loff"][bass.ds(l, 1)].rearrange("o p n -> p (o n)")).then_inc(Z["lrow"], 16)
                sp.dma_start(convw, I["convw"][bass.ds(l, 1)].rearrange("o p (m v) -> p (o m) v", v=4)).then_inc(Z["lrow"], 16)
                for dst, src in ((fw1, I["hy_w1"]), (fw2, I["hy_w2"]), (fb, I["hy_b"]), (hyb, I["hy_bias"])):
                    sp.dma_start(dst[:, :], src[bass.ds(l, 1)].rearrange("o p n -> p (o n)")).then_inc(Z["lfil"], 16)
                last = {}
                for name, (s0, k, free) in LOADS.items():
                    g = GR[1 if name[0] == "s" else 0]
                    for s in range(s0, s0 + k):
                        if s in last:
                            sp.wait_ge(signal(last[s][0], last[s][1]), last[s][2])
                        last[s] = free
                    src, (n, m) = source(name, l)
                    sp.dma_start(slots[:, s0 * SLOT_W:s0 * SLOT_W + n * m].rearrange("p (n m) -> p n m", m=m),
                                 src).then_inc(slot_full[s0], 16)
                    if name[0] == "s" and name[1] == "ukv":
                        sp.wait_ge(of_group["arrived"], 4)
                        sp.sem_clear(range(group_nums[0], group_nums[-1] + 1))
                        sp.sem_inc(go)
                        last = {q: v for q, v in last.items() if v[0] == "s"}
                        sp.dma_start(ckvn[:, 0, :], I["cache_ckv"][bass.ds(l, 1)].rearrange("o p n -> p (o n)")).then_inc(g.s["ctx"], 16)
                        sp.dma_start(krp[:, 0, NOPE:HQ], I["cache_kr"][bass.ds(l, 1)].rearrange("o p n -> p (o n)")).then_inc(g.s["ctx"], 16)
                    if name[0] in ("p", "s") and name[1] == "uq" and not g.latent:
                        sp.wait_ge(g.s["cn"], 1)
                        sp.dma_start(O["ckv"][bass.ds(l, 1)].rearrange("o p n -> p (o n)"), ckvn[:, 0, :]).then_inc(g.s["state"], 16)
                        sp.dma_start(O["kr"][bass.ds(l, 1)].rearrange("o p n -> p (o n)"), krp[:, 0, NOPE:HQ]).then_inc(g.s["state"], 16)
                    if name[0] in ("p", "s") and name[1] == "hy" and name[2] == 3:
                        sp.wait_ge(g.s["attn"], g.nt)
                        sp.wait_ge(g.s["tra"], g.nt)
                        if not g.latent:
                            sp.wait_ge(g.s["state"], 32)
                        sp.dma_start(w3, I["hy_w3"][bass.ds(l, 1)].rearrange("o p n -> p (o n)")).then_inc(Z["lw3a"], 16)
                        sp.dma_start(arena[:, 16384:17408], I["decay"][bass.ds(2 * l, 1)].rearrange("o n -> (o n)").partition_broadcast(128)).then_inc(Z["ldec0"], 16)
                    if name[0] in ("p", "s") and name[1] == "Ms":
                        sp.wait_ge(g.s["win"], 2 * g.nt)
                        sp.dma_start(arena[:, 16384:17408], I["decay"][bass.ds(2 * l + 1, 1)].rearrange("o n -> (o n)").partition_broadcast(128)).then_inc(Z["ldec1"], 16)
                        sp.wait_ge(g.s["U_ps"], g.nt)
                        sp.dma_start(w3, I["hy_w3"][bass.ds(l, 1)].rearrange("o p n -> p (o n)")).then_inc(Z["lw3b"], 16)
                sp.wait_ge(of_group["arrived"], 4)
                sp.sem_clear(range(group_nums[0], group_nums[-1] + 1))
                sp.sem_clear(range(nums[0], nums[-1] + 1))
                sp.sem_inc(go)
            sp.dma_start(arena[:, 0:D], I["final_norm"].partition_broadcast(128)).then_inc(final, 16)
            sp.wait_ge(fch, 1)
            sp.dma_start(O["y"].rearrange("(t p) d -> p t d", p=128), x).then_inc(out_done, 16)
            sp.wait_ge(out_done, 16)

        @block.tensor
        def _(pe):
            busy, used = {}, {}

            def claim(bank, s, value):
                if bank in busy:
                    pe.wait_ge(*busy[bank])
                busy[bank] = (s, value)

            def loaded(name):
                s0, k, _ = LOADS[name]
                order = [n for n in LOADS if LOADS[n][0] == s0]
                pe.wait_ge(slot_full[s0], 16 * (order.index(name) + 1))

            def w3d(name, m, n=8):
                return slot_of(name, n * m).rearrange("p (n m) -> p n m", m=m)

            def adaln():
                claim(7, Z["mod"], 1)
                pe.wait_ge(silu, 4)
                for i in range(24):
                    loaded(("ada", i))
                    w = w3d(("ada", i), 256)
                    for c in (0, 1):
                        for k in range(KD):
                            m = pe.matmul(ps[:, 7, 4 * i + 2 * c:4 * i + 2 * c + 2], w[:, k, c * 128:c * 128 + 128],
                                          cfm[:, 2 * k:2 * k + 2], start=(k == 0), stop=(k == 7))
                    m.then_inc(Z["ada_ps"], 1)

            def dense(g):
                s, nt, T = g.s, g.nt, g.T
                n = g.name
                pe.wait_ge(setup, 16 * 7)
                pe.wait_ge(s["xn"], nt)
                for c in range(KD):
                    claim(c % 4, s["hT1"], c + 1)
                    for j in range(nt):
                        m = pe.transpose(ps[:, c % 4, j * 128:j * 128 + 128], xn[:, j, c * 128:c * 128 + 128], ident[:, :])
                    m.then_inc(s["tr1"], 1)
                loaded((n, "qkv"))
                w = w3d((n, "qkv"), HY0)
                pe.wait_ge(s["hT1"], KD)
                for j in range(nt):
                    for v, (c0, cn) in enumerate(((0, QR), (QR, KVR + ROPE))):
                        b = (2 * j + v) % 4
                        claim(b, s["ss_qkv"], 2 * j + v + 1)
                        for k in range(KD):
                            m = pe.matmul(ps[:, b, 0:cn], hT3[:, k, j * 128:j * 128 + 128], w[:, k, c0:c0 + cn],
                                          start=(k == 0), stop=(k == 7))
                        m.then_inc(s["qkv_ps"], 1)
                pe.wait_ge(s["cn"], nt)
                if g.latent:
                    pe.wait_ge(s["ctx"], 32)
                at = 0
                for c in range(3):
                    claim(4 + at % 4, s["cT"], at + 1)
                    for j in range(nt):
                        m = pe.transpose(ps[:, 4 + at % 4, j * 128:j * 128 + 128], cqn[:, j, c * 128:c * 128 + 128], ident[:, :])
                    m.then_inc(s["trc"], 1)
                    at += 1
                for q in range(g.ckv_banks):
                    claim(4 + at % 4, s["cT"], at + 1)
                    for r in range(4 * q, min(4 * q + 4, 2 * g.nk)):
                        m = pe.transpose(ps[:, 4 + at % 4, (r % 4) * 128:(r % 4) * 128 + 128],
                                         ckvn[:, r % g.nk, (r // g.nk) * 128:(r // g.nk) * 128 + 128], ident[:, :])
                    m.then_inc(s["trc"], 1)
                    at += 1
                for q in range(g.kr_banks):
                    claim(4 + at % 4, s["cT"], at + 1)
                    for r in range(4 * q, min(4 * q + 4, g.nk)):
                        m = pe.transpose(ps[0:HQ, 4 + at % 4, (r % 4) * 128:(r % 4) * 128 + 128], krp[:, r, :], ident[:, :])
                    m.then_inc(s["trc"], 1)
                    at += 1
                loaded((n, "uq"))
                w = w3d((n, "uq"), 768, 3)
                pe.wait_ge(s["cT"], 3)

                def q_proj(j):
                    for v in (0, 1):
                        b = 2 * (j % 2) + v
                        claim(b, s["q_tm"], j + 1)
                        for k in range(3):
                            m = pe.matmul(ps[:, b, 0:QR], cqnT[:, k, j * 128:j * 128 + 128], w[:, k, v * QR:v * QR + QR],
                                          start=(k == 0), stop=(k == 2))
                    m.then_inc(s["q_ps"], 1)

                def q_turn(j):
                    pe.wait_ge(s["q_rope"] if g.latent else s["q_tm"], j + 1)
                    for v in (0, 1):
                        b = 4 + (2 * j + v) % 4
                        claim(b, s["qT"], 2 * j + v + 1)
                        for h in range(4):
                            m = pe.transpose(ps[0:HQ, b, h * 128:h * 128 + 128],
                                             q_tm[:, j % 2, (4 * v + h) * HQ:(4 * v + h + 1) * HQ], ident[:, :])
                        m.then_inc(s["trq"], 1)

                for j in range(nt + 1):
                    if j < nt:
                        q_proj(j)
                    if j >= 1:
                        q_turn(j - 1)
                loaded((n, "ukv"))
                w = w3d((n, "ukv"), 1024, 2)
                pe.wait_ge(s["cT"], 3 + g.ckv_banks)
                ck = ckvT[:, 0:2 * g.TK].rearrange("p (c t) -> p c t", c=2)
                for i, (h0, nh, kt, n_kt) in enumerate(g.k_pieces):
                    b = i % 4
                    claim(b, s["kT"], i + 1)
                    for h in range(nh):
                        for k in (0, 1):
                            m = pe.matmul(ps[0:NOPE, b, h * 128:h * 128 + n_kt * 128], w[:, k, (h0 + h) * 128:(h0 + h) * 128 + NOPE],
                                          ck[:, k, kt * 128:(kt + n_kt) * 128], start=(k == 0), stop=(k == 1))
                    m.then_inc(s["k_ps"], 1)
                for kt in range(g.nk):
                    b = 4 + kt % 4
                    claim(b, s["v"], kt + 1)
                    for k in (0, 1):
                        wv = w[:, k, :].rearrange("p (h c) -> p h c", h=NH)[:, :, NOPE:NOPE + VD]
                        m = pe.matmul(ps[:, b, :].rearrange("p (h c) -> p h c", h=NH), ck[:, k, kt * 128:kt * 128 + 128], wv,
                                      start=(k == 0), stop=(k == 1))
                    m.then_inc(s["v_ps"], 1)
                pe.wait_ge(s["qT"], 2 * nt)
                pe.wait_ge(s["kT"], len(g.k_pieces))
                pe.wait_ge(s["cT"], 3 + g.ckv_banks + g.kr_banks)
                pe.wait_ge(s["v"], g.nk)
                kv, N = KTv(g), nt * NH
                for b in range(8):
                    if b in busy:
                        pe.wait_ge(*busy.pop(b))
                for i in range(N + 2):
                    if i < N:
                        j, h, b = i // NH, i % NH, 2 * (i % 2)
                        claim(b, s["prob"], i + 1)
                        for c0 in range(0, g.TK, 512):
                            cn = min(512, g.TK - c0)
                            m = pe.matmul(psf[:, b * 512 + c0:b * 512 + c0 + cn], qT[0:HQ, h, j * 128:j * 128 + 128],
                                          kv[0:HQ, h, c0:c0 + cn], start=True, stop=True)
                        m.then_inc(s["s_ps"], 1)
                    if 1 <= i <= N:
                        pe.wait_ge(s["prob"], i)
                        claim(4, s["pT"], i)
                        for kt in range(g.nk):
                            m = pe.transpose(psf[:, 4 * 512 + kt * 128:4 * 512 + kt * 128 + 128],
                                             prob[:, (i - 1) % 2, kt * 128:kt * 128 + 128], ident[:, :])
                        m.then_inc(s["trp"], 1)
                    if i >= 2:
                        j, h = (i - 2) // NH, (i - 2) % NH
                        b = 6 + j % 2
                        if h == 0:
                            claim(b, s["attn"], j + 1)
                        pe.wait_ge(s["pT"], i - 1)
                        for kt in range(g.nk):
                            m = pe.matmul(ps[:, b, h * VD:h * VD + VD], probT[:, i % 2, kt * 128:kt * 128 + 128],
                                          V[:, kt, h * VD:h * VD + VD], start=(kt == 0), stop=(kt == g.nk - 1))
                        m.then_inc(s["o_ps"], 1)
                for b in (0, 2, 4, 6, 7):
                    if b in busy:
                        pe.wait_ge(*busy.pop(b))
                for j in range(nt):
                    claim(j % 4, s["aT"], j + 1)
                    pe.wait_ge(s["attn"], j + 1)
                    for c in range(4):
                        m = pe.transpose(ps[:, j % 4, c * 128:c * 128 + 128], attn_all[:, j, c * 128:c * 128 + 128], ident[:, :])
                    m.then_inc(s["tra"], 1)
                for i in range(6):
                    loaded((n, "hy", i))
                    w = w3d((n, "hy", i), 256)
                    for c in (0, 1):
                        mi = 2 * i + c
                        b = 4 + mi % 4
                        claim(b, s["hyc"], mi + 1)
                        for k in range(KD):
                            m = pe.matmul(ps[:, b, 0:T], w[:, k, c * 128:c * 128 + 128], hT3[:, k, 0:T], start=(k == 0), stop=(k == 7))
                        m.then_inc(s["hyc_ps"], 1)
                pe.wait_ge(Z["lfil"], 64)
                z0 = 0 if not g.latent else SEQ
                claim(0, s["f_red"], 1)
                pe.matmul(ps[0:HID, 0, 0:T], fw1[:, :], zT[:, z0:z0 + T], start=True, stop=True).then_inc(s["f_ps"], 1)
                pe.wait_ge(s["f"], 1)
                claim(1, s["f_red"], 2)
                pe.matmul(ps[0:HID, 1, 0:T], fw2[:, :], f1T[:, 0:T], start=True, stop=True).then_inc(s["f_ps"], 1)
                pe.wait_ge(s["f"], 2)

                def spectra(o):
                    w3sem = Z["lw3b"] if o else Z["lw3a"]
                    pe.wait_ge(w3sem, 16 * (g.gi + 1))
                    for tc in range(nt):
                        for d in (0, 1):
                            i = (o * nt + tc) * 2 + d
                            claim(i % 4, s["wh"], i + 1)
                            pe.matmul(ps[:, i % 4, :], f2T[:, tc * 128:tc * 128 + 128], w3[:, (2 * o + d) * HYW:(2 * o + d + 1) * HYW],
                                      start=True, stop=True).then_inc(s["h_ps"], 1)
                    pe.wait_ge(s["sd"], (o + 1) * nt)
                    for r, kind in enumerate(("C", "S")):
                        loaded((n, kind))
                        w = w3d((n, kind), T, nt)
                        for kc in range(nt):
                            i = (o * 2 + r) * nt + kc
                            claim(4 + i % 4, s["K"], i + 1)
                            for tc in range(nt):
                                m = pe.matmul(ps[:, 4 + i % 4, :], w[:, tc, kc * 128:kc * 128 + 128], Yf[:, r, tc, :],
                                              start=(tc == 0), stop=(tc == nt - 1))
                            m.then_inc(s["K_ps"], 1)

                def convolve(o):
                    pe.wait_ge(*((s["y"], 4) if o else (s["hyc"], 12)))
                    for j in range(nt):
                        claim(j % 4, s["u"], o * nt + j + 1)
                        for c in range(4):
                            m = pe.transpose(ps[:, j % 4, c * 128:c * 128 + 128], hyT[:, c, j * 128:j * 128 + 128], ident[:, :])
                        m.then_inc(s["tru"], 1)
                    pe.wait_ge(s["u"], (o + 1) * nt)
                    loaded((n, "Mc"))
                    loaded((n, "Ms"))
                    M = [w3d((n, kind), T, nt) for kind in ("Mc", "Ms")]
                    for kc in range(nt):
                        for r in (0, 1):
                            b = 4 + 2 * (kc % 2) + r
                            claim(b, s["Ym"], o * nt + kc + 1)
                            for tc in range(nt):
                                m = pe.matmul(ps[:, b, :], M[r][:, tc, kc * 128:kc * 128 + 128], u_tm[:, tc, :],
                                              start=(tc == 0), stop=(tc == nt - 1))
                        m.then_inc(s["U_ps"], 1)
                    pe.wait_ge(s["Yc"], (o + 1) * nt)
                    for c in range(4):
                        claim(c, s["y"], o * 4 + c + 1)
                        for r in (0, 1):
                            for kc in range(nt):
                                m = pe.matmul(ps[:, c, 0:T], Yf[:, r, kc, c * 128:c * 128 + 128], M[r][:, kc, 0:T],
                                              start=(r == 0 and kc == 0), stop=(r == 1 and kc == nt - 1))
                        m.then_inc(s["y_ps"], 1)

                for o in (0, 1):
                    spectra(o)
                    convolve(o)
                for r in range(4):
                    pe.wait_ge(s["dgr"], r + 1)
                    for c in (0, 1):
                        claim(4 + (2 * r + c) % 4, s["row"], 2 * r + c + 1)
                        pe.matmul(ps[:, 4 + (2 * r + c) % 4, :], ones[:, :], dgr[:, 4 * c:4 * c + 4, :].rearrange("p n m -> p (n m)"),
                                  start=True, stop=True).then_inc(s["row_ps"], 1)
                pe.wait_ge(s["y"], 8)
                pe.wait_ge(s["aT"], nt)
                for c in range(KD):
                    i, cc = c // 2, (c % 2) * 128
                    for v, kind in enumerate(("ga", "gb", "oa", "ob")):
                        b = 4 * (c % 2) + v
                        claim(b, *((s["th"], 2 * c + v + 1) if v < 2 else (s["mm"], c + 1)))
                        name = (n, kind if v < 2 else "oab", i)
                        loaded(name)
                        w = w3d(name, 256)
                        ks = range(KD) if v < 2 else range(4)
                        for k in ks:
                            if v < 2:
                                lhs, rhs = w[:, k, cc:cc + 128], hT3[:, k, 0:T]
                            else:
                                lhs, rhs = w[:, 4 * (v - 2) + k, cc:cc + 128], (attnT, hyoT)[v - 2][:, k, 0:T]
                            m = pe.matmul(ps[:, b, 0:T], lhs, rhs, start=(k == ks[0]), stop=(k == ks[-1]))
                        m.then_inc(s["mg_ps"], 1)
                pe.wait_ge(s["mg"], KD)
                for i in range(4):
                    loaded((n, "out", i))
                    w = w3d((n, "out", i), 256)
                    for j in range(nt):
                        q = i * nt + j
                        claim(q % 8, s["r2"], q + 1)
                        for k in range(KD):
                            m = pe.matmul(ps[:, q % 8, 0:256], mergedT[:, k, j * 128:j * 128 + 128], w[:, k, :], start=(k == 0), stop=(k == 7))
                        m.then_inc(s["out_ps"], 1)
                pe.wait_ge(s["h2"], nt)
                for c in range(KD):
                    claim(c % 4, s["hT2"], c + 1)
                    for j in range(nt):
                        m = pe.transpose(ps[:, c % 4, j * 128:j * 128 + 128], h2_of(g, j)[:, c * 128:c * 128 + 128], ident[:, :])
                    m.then_inc(s["tr2"], 1)
                pe.wait_ge(s["hT2"], KD)
                for i in range(NHP + 1):
                    if i < NHP:
                        loaded((n, "wq", i // 2))
                        w = w3d((n, "wq", i // 2), 256)
                        b = 4 + i % 2
                        claim(b, s["qh"], i + 1)
                        for k in range(KD):
                            m = pe.matmul(ps[:, b, 0:T], w[:, k, (i % 2) * 128:(i % 2) * 128 + 128], hT3[:, k, 0:T], start=(k == 0), stop=(k == 7))
                        m.then_inc(s["qh_ps"], 1)
                    if i >= 1:
                        if i == 1:
                            loaded((n, "keys"))
                        kt = w3d((n, "keys"), NK, NHP)
                        pe.wait_ge(s["qh"], i)
                        b = 6 + (i - 1) % 2
                        claim(b, s["sc"], i)
                        for j in range(nt):
                            m = pe.matmul(ps[:, b, j * 128:j * 128 + 128], qh[:, (i - 1) % 4, j * 128:j * 128 + 128], kt[:, i - 1, :],
                                          start=True, stop=True)
                        m.then_inc(s["sc_ps"], 1)

            def experts(g):
                for b in (0, 1):
                    if b in busy:
                        pe.wait_ge(*busy.pop(b))
                n0 = g.t0 * ITERS

                def tile(t):
                    pe.wait_ge(Z["acc_read"], t + 1)
                    for c in (0, 1):
                        pe.matmul(ps[:, c, :], zeros[:, :], zeros[:, :].unsqueeze(1).to_broadcast([128, 4, 128]), start=True, stop=False, skip_group_check=True)
                    with pe.Fori(0, ITERS) as i:
                        for hf in (0, 1):
                            m4 = ((t * ITERS + i) * 2 + hf) * HALF
                            for b in range(HALF):
                                q = hf * HALF + b
                                pe.wait_ge(Z["diag"], m4 + b + 1)
                                for c in (0, 1):
                                    m = pe.matmul(ps[:, c, :], dge[:, q, :], gbuf[:, q, D + c * 512:D + c * 512 + 512],
                                                  start=False, stop=False, skip_group_check=True)
                                m.then_inc(Z["buf_free"], 1)
                if g.latent:
                    with pe.Fori(1, TILES) as t:
                        tile(t)
                else:
                    tile(0)

            with pe.Fori(0, DEPTH) as l:
                busy.clear()
                adaln()
                for g in GR:
                    if g.latent:
                        meet(pe, 2 * l + 1)
                        busy.clear()
                    dense(g)
                for g in GR:
                    experts(g)
                meet(pe, 2 * l + 2)

        @block.scalar
        def _(act):
            done = [0]

            act.wait_ge(setup, 16 * 7)
            act.activation(cth[:, :], cfm[:, :], ACT.Tanh, scale=0.5).then_inc(silu, 1)

            def dense(g):
                s, nt, T = g.s, g.nt, g.T
                for j in range(nt):
                    if j:
                        act.wait_ge(s["ss1"], j)
                    act.activation(junk, x[:, g.t0 + j, :], ACT.Square, accum_out=st[:, j:j + 1]).then_inc(s["ss1"], 1)
                act.wait_ge(Z["mod"], 4)
                for c in range(KD):
                    act.wait_ge(s["tr1"], c + 1)
                    act.activation(hT3[:, c, 0:T], ps[:, c % 4, 0:T], ACT.Identity, scale=fold[:, 0, c, g.gi:g.gi + 1],
                                   bias=mod[:, c, g.gi:g.gi + 1]).then_inc(s["hT1"], 1)
                for j in range(nt):
                    for v, (dst, w, sq) in enumerate(((cqraw, QR, QR), (kvraw, KVR + ROPE, KVR))):
                        i = 2 * j + v
                        act.wait_ge(s["qkv_ps"], i + 1)
                        act.activation(dst[:, j, 0:w], ps[:, i % 4, 0:w], ACT.Copy).then_inc(s["qkv_raw"], 1)
                        if i:
                            act.wait_ge(s["ss_qkv"], i)
                        act.activation(junk[:, 0:sq], ps[:, i % 4, 0:sq], ACT.Square, accum_out=st[:, 8 + v * nt + j:9 + v * nt + j]).then_inc(s["ss_qkv"], 1)
                at = 0
                for c in range(3):
                    act.wait_ge(s["trc"], at + 1)
                    act.activation(cqnT[:, c, 0:T], ps[:, 4 + at % 4, 0:T], ACT.Copy).then_inc(s["cT"], 1)
                    at += 1
                for q in range(g.ckv_banks):
                    w = (min(4 * q + 4, 2 * g.nk) - 4 * q) * 128
                    act.wait_ge(s["trc"], at + 1)
                    act.activation(ckvT[:, q * 512:q * 512 + w], ps[:, 4 + at % 4, 0:w], ACT.Copy).then_inc(s["cT"], 1)
                    at += 1
                for q in range(g.kr_banks):
                    w = (min(4 * q + 4, g.nk) - 4 * q) * 128
                    act.wait_ge(s["trc"], at + 1)
                    src = ps[NOPE:HQ, 4 + at % 4:5 + at % 4, 0:w].to_broadcast([ROPE, NH, w])
                    act.activation(KTv(g)[NOPE:HQ, :, q * 512:q * 512 + w], src, ACT.Copy).then_inc(s["cT"], 1)
                    at += 1
                for j in range(nt):
                    act.wait_ge(s["q_ps"], j + 1)
                    if j >= 2:
                        act.wait_ge(s["trq"], 2 * (j - 1))
                    b = 2 * (j % 2)
                    act.activation(q_tm[:, j % 2, :].rearrange("p (v c) -> p v c", v=2), ps[:, b:b + 2, 0:QR], ACT.Copy,
                                   scale=HQ ** -0.5).then_inc(s["q_tm"], 1)
                for kt in range(g.nk):
                    act.wait_ge(s["v_ps"], kt + 1)
                    act.activation(V[:, kt, :], ps[:, 4 + kt % 4, :], ACT.Copy).then_inc(s["v"], 1)
                for i in range(nt * NH):
                    act.wait_ge(s["smax"], i + 1)
                    if i >= 2:
                        act.wait_ge(s["trp"], i - 1)
                    b = 2 * (i % 2)
                    act.activation(prob[:, i % 2, 0:g.TK], psf[:, b * 512:b * 512 + g.TK], ACT.Exp, bias=nmax[:, i % 4:i % 4 + 1],
                                   accum_out=ssum[:, i:i + 1]).then_inc(s["prob"], 1)
                    if i >= 1:
                        turned(g, i - 1)
                turned(g, nt * NH - 1)
                for j in range(nt):
                    act.wait_ge(s["tra"], j + 1)
                    act.activation(attnT[:, :, j * 128:j * 128 + 128], ps[:, j % 4, :].rearrange("p (c t) -> p c t", c=4), ACT.Copy).then_inc(s["aT"], 1)
                act.wait_ge(Z["lrow"], 64)
                act.wait_ge(s["tra"], nt)
                if not g.latent:
                    act.wait_ge(s["state"], 32)
                for m in range(12):
                    act.wait_ge(s["hyc_ps"], m + 1)
                    act.activation(hyT[:, m, 0:T], ps[:, 4 + m % 4, 0:T], ACT.Identity, scale=convw[:, m, 1:2], bias=convw[:, m, 3:4]).then_inc(s["hyc_mid"], 1)
                for i in (0, 1):
                    act.wait_ge(s["f_red"], i + 1)
                    act.activation((f1T, f2T)[i][:, 0:T], ftmp[0:HID, 2, 0:T], ACT.Sin).then_inc(s["f"], 1)
                for o in (0, 1):
                    if o:
                        act.wait_ge(s["Yc"], nt)
                        act.wait_ge(Z["ldec1"], 16 * (g.gi + 1))
                    else:
                        act.wait_ge(Z["ldec0"], 16 * (g.gi + 1))
                    for tc in range(nt):
                        for d in (0, 1):
                            i = (o * nt + tc) * 2 + d
                            if i >= 2:
                                act.wait_ge(s["wh"], i - 1)
                            act.activation(win[:, i % 2, :], decay[:, d, :], ACT.Exp, scale=negt[:, g.t0 + tc:g.t0 + tc + 1]).then_inc(s["win"], 1)
                    for i in range(2 * nt):
                        i += o * 2 * nt
                        act.wait_ge(s["K_ps"], i + 1)
                        act.activation(Kf[:, (i // nt) % 2, i % nt, :], ps[:, 4 + i % 4, :], ACT.Copy).then_inc(s["K"], 1)
                    for j in range(nt):
                        act.wait_ge(s["tru"], o * nt + j + 1)
                        act.activation(u_tm[:, j, :], ps[:, j % 4, :], ACT.Copy).then_inc(s["u"], 1)
                for r in range(4):
                    for c in (0, 1):
                        act.wait_ge(s["row_ps"], 2 * r + c + 1)
                        dst = rows[:, r, c * 512:c * 512 + 512] if r < 3 else g2[:, g.gi, c * 512:c * 512 + 512]
                        act.activation(dst, ps[:, 4 + (2 * r + c) % 4, :], ACT.Copy).then_inc(s["row"], 1)
                for c in range(KD):
                    for v in (0, 1):
                        act.wait_ge(s["mg_ps"], 4 * c + v + 1)
                        if c >= 2:
                            act.wait_ge(s["mm"], c - 1)
                        act.activation(tg[:, 2 * (c % 2) + v, 0:T], ps[:, 4 * (c % 2) + v, 0:T], ACT.Tanh, scale=0.5).then_inc(s["th"], 1)
                act.wait_ge(s["xadd"], 4 * nt)
                for j in range(nt):
                    if j:
                        act.wait_ge(s["ss2"], j)
                    act.activation(junk, x[:, g.t0 + j, :], ACT.Square, accum_out=st[:, j:j + 1]).then_inc(s["ss2"], 1)
                for c in range(KD):
                    act.wait_ge(s["tr2"], c + 1)
                    act.activation(hT3[:, c, 0:T], ps[:, c % 4, 0:T], ACT.Copy).then_inc(s["hT2"], 1)
                for i in range(NHP):
                    act.wait_ge(s["qh_ps"], i + 1)
                    if i >= 4:
                        act.wait_ge(s["sc_ps"], i - 3)
                    act.activation(qh[:, i % 4, 0:T], ps[:, 4 + i % 2, 0:T], ACT.Copy).then_inc(s["qh"], 1)
                for j in range(nt):
                    act.wait_ge(s["top"], j + 1)
                    act.activation(gex, gex, ACT.Exp).then_inc(s["ge"], 1)

            def turned(g, i):
                act.wait_ge(g.s["trp"], i + 1)
                if i >= 2:
                    act.wait_ge(g.s["o_ps"], i - 1)
                act.activation(probT[:, i % 2, 0:g.TK], psf[:, 4 * 512:4 * 512 + g.TK], ACT.Copy).then_inc(g.s["pT"], 1)

            def experts(g):
                def tile(t):
                    with act.Fori(0, ITERS) as i:
                        for hf in (0, 1):
                            m = (t * ITERS + i) * 2 + hf
                            q = hf * HALF
                            act.wait_ge(Z["inner"], m + 1)
                            act.activation(dth[:, q:q + HALF], din[:, q:q + HALF], ACT.Tanh, scale=GELU_C).then_inc(Z["th_e"], 1)
                            act.wait_ge(Z["w_ready"], m + 1)
                            act.wait_ge(Z["buf_free"], HALF * (m + 1))
                            for b in range(HALF):
                                act.activation(dge[:, q + b, :], ident[:, :], ACT.Copy, scale=dw[:, q + b:q + b + 1]).then_inc(Z["diag"], 1)
                if g.latent:
                    with act.Fori(1, TILES) as t:
                        tile(t)
                else:
                    tile(0)

            with act.Fori(0, DEPTH) as l:
                for g in GR:
                    if g.latent:
                        meet(act, 2 * l + 1)
                    dense(g)
                act.wait_ge(GR[1].s["gw"], 4)
                for g in GR:
                    experts(g)
                meet(act, 2 * l + 2)
            for j in range(TILES):
                if j:
                    act.wait_ge(final_sq, j)
                act.activation(junk, x[:, j, :], ACT.Square, accum_out=st[:, j:j + 1]).then_inc(final_sq, 1)

        @block.vector
        def _(dve):
            count = [0]

            def link(ins):
                count[0] += 1
                ins.then_inc(Z["chain"], 1)
                dve.wait_ge(Z["chain"], count[0])

            def rsqrt(cols, n, chain_link):
                v, y, t = st[:, cols:cols + n], st[:, 32:32 + n], st[:, 48:48 + n]
                chain_link(dve.tensor_scalar(t.bitcast(i32), v.bitcast(i32), 1, None, ALU.logical_shift_right))
                chain_link(dve.tensor_scalar(y.bitcast(i32), t.bitcast(i32), -1.0, 1597463007.0, ALU.mult, ALU.add))
                chain_link(dve.tensor_scalar(v, v, -0.5, None, ALU.mult))
                for _ in range(4):
                    chain_link(dve.tensor_tensor(t, y, y, ALU.mult))
                    chain_link(dve.tensor_tensor(t, t, v, ALU.mult))
                    chain_link(dve.scalar_tensor_tensor(out=y, in0=t, scalar=1.5, in1=y, op0=ALU.add, op1=ALU.mult))

            def mod_vectors():
                dve.wait_ge(Z["lvec"], 16)
                dve.wait_ge(Z["ada_ps"], 24)
                bias = lvec[:, 0:48].unsqueeze(2).to_broadcast([128, 48, 2])
                dve.tensor_tensor(mod, ps[:, 7, 0:96].rearrange("p (c g) -> p c g", g=2), bias, ALU.add).then_inc(Z["mod"], 1)
                dve.wait_ge(Z["mod"], 1)
                for v, c0 in ((0, 8), (1, 32)):
                    nrm = lvec[:, 48 + 8 * v:56 + 8 * v].unsqueeze(2).to_broadcast([128, 8, 2])
                    dve.scalar_tensor_tensor(out=fold[:, v, :, :], in0=mod[:, c0:c0 + 8, :], scalar=1.0, in1=nrm,
                                             op0=ALU.add, op1=ALU.mult).then_inc(Z["mod"], 1)
                dve.tensor_scalar(fold[:, 2, :, :], mod[:, 16:24, :], 0.5, None, ALU.mult).then_inc(Z["mod"], 1)
                dve.wait_ge(Z["mod"], 4)

            def dense(g):
                s, nt, T = g.s, g.nt, g.T

                def mean(cols, n, width):
                    link(dve.tensor_scalar(st[:, cols:cols + n], st[:, cols:cols + n], 1.0 / width, EPS, ALU.mult, ALU.add))

                dve.wait_ge(s["ss1"], nt)
                mean(0, nt, D)
                rsqrt(0, nt, link)
                for j in range(nt):
                    dve.tensor_scalar(xn[:, j, :], x[:, g.t0 + j, :], st[:, 32 + j:33 + j], None, ALU.mult).then_inc(s["xn"], 1)
                dve.wait_ge(s["ss_qkv"], 2 * nt)
                mean(8, nt, QR)
                mean(8 + nt, nt, KVR)
                rsqrt(8, 2 * nt, link)
                dve.wait_ge(Z["lrow"], 64)
                dve.wait_ge(setup, 16 * 7)
                k0 = g.nk - nt
                for j in range(nt):
                    dve.scalar_tensor_tensor(out=cqn[:, j, :], in0=cqraw[:, j, :], scalar=st[:, 32 + j:33 + j], in1=qn_row[:, :],
                                             op0=ALU.mult, op1=ALU.mult)
                    dve.scalar_tensor_tensor(out=ckvn[:, k0 + j, :], in0=kvraw[:, j, 0:KVR], scalar=st[:, 32 + nt + j:33 + nt + j],
                                             in1=kvn_row[:, :], op0=ALU.mult, op1=ALU.mult)
                    kr = kvraw[:, j, KVR:KVR + ROPE]
                    dst = krp[:, k0 + j, NOPE:HQ]
                    if g.latent:
                        c, sn = trig[:, 0, j, :], trig[:, 1, j, :]
                        ta, tb = rope_tmp[:, 64 * j:64 * j + 32], rope_tmp[:, 64 * j + 32:64 * j + 64]
                        dve.tensor_tensor(ta, kr, c, ALU.mult)
                        dve.tensor_tensor(tb[:, 0:16], kr[:, 16:32], sn[:, 0:16], ALU.mult)
                        link(dve.tensor_tensor(tb[:, 16:32], kr[:, 0:16], sn[:, 16:32], ALU.mult))
                        dve.tensor_tensor(dst, ta, tb, ALU.add).then_inc(s["cn"], 1)
                    else:
                        dve.tensor_copy(dst, kr).then_inc(s["cn"], 1)

                def q_to_heads(i):
                    j, v = i // 2, i % 2
                    dve.wait_ge(s["trq"], i + 1)
                    dve.tensor_copy(qT[0:HQ, 4 * v:4 * v + 4, j * 128:j * 128 + 128],
                                    ps[0:HQ, 4 + i % 4, :].rearrange("p (h t) -> p h t", h=4)).then_inc(s["qT"], 1)

                for j in range(nt):
                    if g.latent:
                        dve.wait_ge(s["q_tm"], j + 1)
                        dve.wait_ge(*((s["q_rope"], j) if j else (s["cn"], nt)))
                        qv = q_tm[:, j % 2, :].rearrange("p (h c) -> p h c", c=HQ)
                        c, sn = (trig[:, v:v + 1, j, :].to_broadcast([128, NH, ROPE]) for v in (0, 1))
                        ta, tb = (rope_tmp[:, v * 256:v * 256 + 256].rearrange("p (h c) -> p h c", h=NH) for v in (0, 1))
                        dve.tensor_tensor(ta, qv[:, :, NOPE:HQ], c, ALU.mult)
                        dve.tensor_tensor(tb[:, :, 0:16], qv[:, :, NOPE + 16:HQ], sn[:, :, 0:16], ALU.mult)
                        link(dve.tensor_tensor(tb[:, :, 16:32], qv[:, :, NOPE:NOPE + 16], sn[:, :, 16:32], ALU.mult))
                        dve.tensor_tensor(qv[:, :, NOPE:HQ], ta, tb, ALU.add).then_inc(s["q_rope"], 1)
                    if j >= 1:
                        q_to_heads(2 * j - 2)
                        q_to_heads(2 * j - 1)
                q_to_heads(2 * nt - 2)
                q_to_heads(2 * nt - 1)
                for i, (h0, nh, kt, n_kt) in enumerate(g.k_pieces):
                    dve.wait_ge(s["k_ps"], i + 1)
                    w = nh * n_kt * 128
                    dve.tensor_copy(KTv(g)[0:NOPE, h0:h0 + nh, kt * 128:(kt + n_kt) * 128],
                                    ps[0:NOPE, i % 4, 0:w].rearrange("p (h t) -> p h t", h=nh)).then_inc(s["kT"], 1)

                def normalise(j):
                    dve.wait_ge(s["o_ps"], NH * (j + 1))
                    link(dve.reciprocal(ssum[:, 32 + 8 * (j % 2):40 + 8 * (j % 2)], ssum[:, NH * j:NH * j + NH]))
                    den = ssum[:, 32 + 8 * (j % 2):40 + 8 * (j % 2)].unsqueeze(2).to_broadcast([128, NH, VD])
                    dve.tensor_tensor(attn_all[:, j, :].rearrange("p (h c) -> p h c", h=NH),
                                      ps[:, 6 + j % 2, :].rearrange("p (h c) -> p h c", h=NH), den, ALU.mult).then_inc(s["attn"], 1)

                for i in range(nt * NH):
                    dve.wait_ge(s["s_ps"], i + 1)
                    if i >= 4:
                        dve.wait_ge(s["prob"], i - 3)
                    b = 2 * (i % 2)
                    dve.tensor_reduce(nmax[:, i % 4:i % 4 + 1], psf[:, b * 512:b * 512 + g.TK], AX.X, ALU.max, negate=True).then_inc(s["smax"], 1)
                    if i >= NH + 3 and (i - 3) % NH == 0:
                        normalise((i - 3) // NH - 1)
                normalise(nt - 1)
                dve.wait_ge(Z["lrow"], 64)
                for m in range(12):
                    b = 4 + m % 4
                    dve.wait_ge(s["hyc_mid"], m + 1)
                    link(dve.scalar_tensor_tensor(out=hyT[:, m, 1:T], in0=ps[:, b, 0:T - 1], scalar=convw[:, m, 0:1], in1=hyT[:, m, 1:T],
                                                  op0=ALU.mult, op1=ALU.add))
                    dve.scalar_tensor_tensor(out=hyT[:, m, 0:T - 1], in0=ps[:, b, 1:T], scalar=convw[:, m, 2:3], in1=hyT[:, m, 0:T - 1],
                                             op0=ALU.mult, op1=ALU.add).then_inc(s["hyc"], 1)
                dve.wait_ge(Z["lfil"], 64)
                for i in (0, 1):
                    dve.wait_ge(s["f_ps"], i + 1)
                    if i:
                        dve.wait_ge(s["f"], 1)
                    fa, fn, fr = (ftmp[0:HID, v, 0:T] for v in range(3))
                    link(dve.tensor_scalar(fa, ps[0:HID, i, 0:T], fb[:, i:i + 1], None, ALU.add))
                    link(dve.tensor_scalar(fn, fa, 1.0 / (2 * math.pi), MAGIC, ALU.mult, ALU.add))
                    link(dve.tensor_scalar(fn, fn, -MAGIC, None, ALU.add))
                    link(dve.scalar_tensor_tensor(out=fr, in0=fn, scalar=-TWO_PI_HI, in1=fa, op0=ALU.mult, op1=ALU.add))
                    link(dve.scalar_tensor_tensor(out=fr, in0=fn, scalar=-TWO_PI_LO, in1=fr, op0=ALU.mult, op1=ALU.add))
                    dve.tensor_scalar(fr, fr, 3.1415925, -3.1415925, ALU.min, ALU.max).then_inc(s["f_red"], 1)
                for o in (0, 1):
                    for i in range(o * 2 * nt, (o + 1) * 2 * nt):
                        dve.wait_ge(s["h_ps"], i + 1)
                        dve.wait_ge(s["win"], i + 1)
                        if i >= 4:
                            dve.wait_ge(s["sd"], i // 2 - 1)
                        dve.tensor_tensor(wh[:, i % 4, :], ps[:, i % 4, :], win[:, i % 2, :], ALU.mult).then_inc(s["wh"], 1)
                    for kc in range(nt):
                        i = o * nt + kc
                        dve.wait_ge(s["U_ps"], i + 1)
                        dve.wait_ge(s["K"], (o + 1) * 2 * nt)
                        if kc >= 2:
                            dve.wait_ge(s["Yc"], i - 1)
                        b = 4 + 2 * (kc % 2)
                        for v, (ur, kr) in enumerate(((0, 0), (1, 1), (0, 1), (1, 0))):
                            m = dve.tensor_tensor(prodm[:, kc % 2, v, :], ps[:, b + ur, :], Kf[:, kr, kc, :], ALU.mult)
                        m.then_inc(s["Ym"], 1)
                    for c in range(4):
                        dve.wait_ge(s["y_ps"], 4 * o + c + 1)
                        dst = hyT[:, c, 0:T] if o == 0 else hyoT[:, c, 0:T]
                        dve.scalar_tensor_tensor(out=dst, in0=ps[:, c, 0:T], scalar=1.0 / T, in1=hyT[:, 4 * (o + 1) + c, 0:T],
                                                 op0=ALU.mult, op1=ALU.mult).then_inc(s["y"], 1)
                ident3 = ident[:, :].unsqueeze(1).to_broadcast([128, 8, 128])
                for r, vec in enumerate((fold[:, 2, :, g.gi], fold[:, 1, :, g.gi], mod[:, 24:32, g.gi], mod[:, 40:48, g.gi])):
                    if r:
                        dve.wait_ge(s["row_ps"], 2 * r)
                    dve.tensor_tensor(dgr, ident3, vec.unsqueeze(2).to_broadcast([128, 8, 128]), ALU.mult).then_inc(s["dgr"], 1)
                for c in range(KD):
                    for v in (0, 1):
                        dve.wait_ge(s["th"], 2 * c + v + 1)
                        dve.wait_ge(s["mg_ps"], 4 * c + 3 + v)
                        if c >= 2:
                            dve.wait_ge(s["mg"], c - 1)
                        m = dve.scalar_tensor_tensor(out=mtmp[:, 2 * (c % 2) + v, 0:T], in0=tg[:, 2 * (c % 2) + v, 0:T], scalar=1.0,
                                                     in1=ps[:, 4 * (c % 2) + 2 + v, 0:T], op0=ALU.add, op1=ALU.mult)
                    m.then_inc(s["mm"], 1)
                dve.wait_ge(s["row"], 8)
                for q in range(4 * nt):
                    i = q // nt
                    dve.wait_ge(s["out_ps"], q + 1)
                    if q >= 2:
                        dve.wait_ge(s["xadd"], q - 1)
                    dve.tensor_tensor(otmp[:, q % 2, :], ps[:, q % 8, 0:256], rows[:, 0, i * 256:i * 256 + 256], ALU.mult).then_inc(s["r2"], 1)
                dve.wait_ge(s["ss2"], nt)
                mean(0, nt, D)
                rsqrt(0, nt, link)
                for j in range(nt):
                    link(dve.scalar_tensor_tensor(out=xn2[:, j, :], in0=x[:, g.t0 + j, :], scalar=st[:, 32 + j:33 + j], in1=rows[:, 1, :],
                                                  op0=ALU.mult, op1=ALU.mult))
                    dve.tensor_tensor(h2_of(g, j), xn2[:, j, :], rows[:, 2, :], ALU.add).then_inc(s["h2"], 1)
                for i in range(NHP):
                    dve.wait_ge(s["sc_ps"], i + 1)
                    dve.tensor_copy(scores[:, 0:nt, i, :], ps[:, 6 + i % 2, 0:T].rearrange("p (j n) -> p j n", j=nt)).then_inc(s["sc"], 1)
                dve.wait_ge(s["sc"], NHP)
                for j in range(nt):
                    route(g, j)

            def step(instrs):
                link(instrs[-1])

            def route(g, j):
                s, t = g.s, g.t0 + j
                step([dve.max(s16[:, h, 0:8], scores[:, j, h, :]) for h in range(NHP)])
                step([dve.match_replace(scr[:, h, :], s16[:, h, 0:8], scores[:, j, h, :], -3.0e38) for h in range(NHP)])
                step([dve.max(s16[:, h, 8:16], scr[:, h, :]) for h in range(NHP)])
                i16u = i16.bitcast(u32)
                for h in range(NHP):
                    dve.max_index(i16u[:, h, 0:8], s16[:, h, 0:8], scores[:, j, h, :])
                step([dve.max_index(i16u[:, h, 8:16], s16[:, h, 8:16], scr[:, h, :]) for h in range(NHP)])
                link(dve.tensor_copy(i16f, i16u))
                v4 = i16f.rearrange("p (h v) k -> p h v k", v=2)
                link(dve.tensor_scalar(v4[:, :, 0, :], v4[:, :, 0, :], float(NK), None, ALU.mult))
                w4 = s16.rearrange("p (h v) k -> p h v k", v=2)
                at = 0
                for i0, n, w in RUNS:
                    for src, dst in ((w4, cand), (v4, cidx)):
                        out = dst[:, :, at:at + n * w].rearrange("p h (n w) -> p h n w", w=w)
                        m = dve.tensor_tensor(out, src[:, :, 0, i0:i0 + n].unsqueeze(3).to_broadcast([128, PH, n, w]),
                                              src[:, :, 1, 0:w].unsqueeze(2).to_broadcast([128, PH, n, w]), ALU.add)
                    at += n * w
                link(m)
                step([dve.max(top[:, h, 0:8], cand[:, h, :]) for h in range(PH)])
                step([dve.match_replace(scr2[:, h, :], top[:, h, 0:8], cand[:, h, :], -3.0e38) for h in range(PH)])
                step([dve.max(top[:, h, 8:16], scr2[:, h, :]) for h in range(PH)])
                if j:
                    dve.wait_ge(s["gw"], j)
                dve.tensor_tensor(gex, top, top[:, :, 0:1].to_broadcast([128, PH, 16]), ALU.subtract).then_inc(s["top"], 1)
                posu = pos.bitcast(u32)
                for h in range(PH):
                    dve.max_index(posu[:, h, 0:8], top[:, h, 0:8], cand[:, h, :])
                step([dve.max_index(posu[:, h, 8:16], top[:, h, 8:16], scr2[:, h, :]) for h in range(PH)])
                link(dve.tensor_copy(posf, posu))
                full = [128, 16, NC]
                for h in range(PH):
                    m = dve.tensor_tensor(eq[:, h], posf[:, h, :].unsqueeze(2).to_broadcast(full), iota[:, :].unsqueeze(1).to_broadcast(full), ALU.is_equal)
                link(m)
                for h in range(PH):
                    m = dve.tensor_tensor(eq[:, h], eq[:, h], cidx[:, h, :].unsqueeze(1).to_broadcast(full), ALU.mult)
                link(m)
                link(dve.tensor_reduce(posf, eq, AX.X, ALU.add))
                dve.tensor_scalar(idx[:, t * SLOTS:(t + 1) * SLOTS].rearrange("p (h k) -> p h k", h=PH), posf, loff[:, 0:1], None, ALU.add)
                dve.wait_ge(s["ge"], j + 1)
                link(dve.tensor_reduce(gsum, gex, AX.X, ALU.add))
                link(dve.reciprocal(gsum, gsum))
                link(dve.tensor_scalar(gsum, gsum, 0.5, None, ALU.mult))
                dve.tensor_tensor(gwt[:, t * SLOTS:(t + 1) * SLOTS].rearrange("p (h k) -> p h k", h=PH), gex,
                                  gsum.unsqueeze(2).to_broadcast([128, PH, 16]), ALU.mult).then_inc(s["gw"], 1)

            def experts(g, l):
                def tile(t):
                    if g.latent:
                        h2 = h2c
                        dve.tensor_copy(h2c, keep[:, bass.ds((t - 1) * D, D)]).then_inc(Z["h2c"], 1)
                    else:
                        h2 = h2p[:, :]
                    with dve.Fori(0, ITERS) as i:
                        if g.latent:
                            dve.wait_ge(Z["h2c"], t)
                        for hf in (0, 1):
                            n = t * ITERS + i
                            m = n * 2 + hf
                            q = hf * HALF
                            for b in range(HALF):
                                dve.wait_ge(gath[q + b], (l * (TILES * ITERS) + n + 1) * 16)
                                dve.tensor_tensor_reduce(gbuf[:, q + b, 0:D], gbuf[:, q + b, 0:D], h2, 1.0, 0.0, ALU.mult, ALU.add,
                                                         dots[:, q + b:q + b + 1]).then_inc(Z["ttr"], 1)
                            dv, sq, inn, th, w = (v[:, q:q + HALF] for v in (dots, dsq, din, dth, dw))
                            dve.wait_ge(Z["ttr"], m * HALF + HALF)
                            dve.tensor_tensor(sq, dv, dv, ALU.mult).then_inc(Z["p_small"], 1)
                            dve.wait_ge(Z["p_small"], m * 3 + 1)
                            dve.tensor_scalar(sq, sq, GELU_A, 1.0, ALU.mult, ALU.add).then_inc(Z["p_small"], 1)
                            dve.wait_ge(Z["p_small"], m * 3 + 2)
                            dve.tensor_tensor(inn, sq, dv, ALU.mult).then_inc(Z["inner"], 1)
                            dve.wait_ge(Z["th_e"], m + 1)
                            dve.scalar_tensor_tensor(out=w, in0=th, scalar=1.0, in1=dv, op0=ALU.add, op1=ALU.mult).then_inc(Z["p_small"], 1)
                            dve.wait_ge(Z["p_small"], m * 3 + 3)
                            dve.tensor_tensor(w, w, gwt[:, bass.ds(n * NB + q, HALF)], ALU.mult).then_inc(Z["w_ready"], 1)
                    dve.wait_ge(Z["buf_free"], NB + SLOTS * (t + 1))
                    dve.tensor_tensor(eacc, ps[:, 0:2, :].rearrange("p b n -> p (b n)"), g2[:, g.gi, :], ALU.mult).then_inc(Z["acc_read"], 1)
                    dve.wait_ge(Z["acc_read"], t + 2)
                    xt = xflat[:, bass.ds(t * D, D)] if g.latent else xflat[:, 0:D]
                    dve.tensor_tensor(xt, xt, eacc, ALU.add).then_inc(Z["pchain"], 1)
                    dve.wait_ge(Z["pchain"], t + 1)
                if g.latent:
                    with dve.Fori(1, TILES) as t:
                        tile(t)
                else:
                    tile(0)

            dve.memset(krp, 0.0).then_inc(silu, 1)
            dve.memset(ones[:, :], 1.0)
            dve.memset(zeros[:, :], 0.0)
            dve.wait_ge(silu, 2)
            dve.scalar_tensor_tensor(out=cth[:, :], in0=cth[:, :], scalar=1.0, in1=cfm[:, :], op0=ALU.add, op1=ALU.mult).then_inc(silu, 1)
            dve.wait_ge(silu, 3)
            dve.tensor_scalar(cfm[:, :], cth[:, :], 0.5, None, ALU.mult).then_inc(silu, 1)
            with dve.Fori(0, DEPTH) as l:
                count[0] = 0
                mod_vectors()
                for g in GR:
                    if g.latent:
                        meet(dve, 2 * l + 1)
                    dense(g)
                dve.wait_ge(GR[1].s["gw"], 4)
                dve.tensor_copy(zeros[:, :], zeros[:, :]).then_inc(Z["acc_read"], 1)
                for g in GR:
                    experts(g, l)
                meet(dve, 2 * l + 2)
            fc = [0]

            def flink(ins):
                fc[0] += 1
                ins.then_inc(silu, 1)
                dve.wait_ge(silu, 4 + fc[0])
            dve.wait_ge(final, 16)
            dve.wait_ge(final_sq, TILES)
            flink(dve.tensor_scalar(st[:, 0:TILES], st[:, 0:TILES], 1.0 / D, EPS, ALU.mult, ALU.add))
            rsqrt(0, TILES, flink)
            for j in range(TILES):
                m = dve.scalar_tensor_tensor(out=x[:, j, :], in0=x[:, j, :], scalar=st[:, 32 + j:33 + j], in1=arena[:, 0:D],
                                             op0=ALU.mult, op1=ALU.mult)
            m.then_inc(fch, 1)

        @block.gpsimd
        def _(pool):
            def dense(g):
                s, nt, T = g.s, g.nt, g.T
                done = [0]
                for o in (0, 1):
                    pool.wait_ge(Z["lfil"], 64)
                    for tc in range(nt):
                        i = o * nt + tc
                        pool.wait_ge(s["wh"], 2 * i + 2)
                        if o and tc == 0:
                            pool.wait_ge(s["y_ps"], 4)
                        wf, wb = wh[:, (2 * i) % 4, :], wh[:, (2 * i + 1) % 4, :]
                        if tc == 0:
                            pool.tensor_tensor(Yf[:, 0, tc, :], wf, wb, ALU.add).then_inc(s["bias0"], 1)
                            pool.wait_ge(s["bias0"], o + 1)
                            pool.tensor_tensor(Yf[0:1, 0, 0, :], Yf[0:1, 0, 0, :], hyb[:, o * HYW:(o + 1) * HYW], ALU.add)
                        else:
                            pool.tensor_tensor(Yf[:, 0, tc, :], wf, wb, ALU.add)
                        pool.tensor_tensor(Yf[:, 1, tc, :], wf, wb, ALU.subtract).then_inc(s["sd"], 1)
                    for kc in range(nt):
                        i = o * nt + kc
                        pool.wait_ge(s["Ym"], i + 1)
                        pool.wait_ge(s["K_ps"], (o + 1) * 2 * nt)
                        pr = prodm[:, kc % 2]
                        pool.tensor_tensor(Yf[:, 0, kc, :], pr[:, 0, :], pr[:, 1, :], ALU.subtract)
                        pool.tensor_tensor(Yf[:, 1, kc, :], pr[:, 2, :], pr[:, 3, :], ALU.add).then_inc(s["Yc"], 1)
                for c in range(KD):
                    pool.wait_ge(s["mm"], c + 1)
                    mv = mtmp[:, 2 * (c % 2):2 * (c % 2) + 2, 0:T]
                    pool.tensor_tensor(mergedT[:, c, 0:T], mv[:, 0, :], mv[:, 1, :], ALU.add).then_inc(s["mg"], 1)
                for q in range(4 * nt):
                    i, j = q // nt, q % nt
                    pool.wait_ge(s["r2"], q + 1)
                    xv = x[:, g.t0 + j, i * 256:i * 256 + 256]
                    pool.tensor_tensor(xv, xv, otmp[:, q % 2, :], ALU.add).then_inc(s["xadd"], 1)

            def experts(g):
                def tile(t):
                    with pool.Fori(0, ITERS) as i:
                        for hf in (0, 1):
                            n = t * ITERS + i
                            m = n * 2 + hf
                            q = hf * HALF
                            pool.wait_ge(Z["buf_free"], HALF * m + 1)
                            pool.tensor_copy(estage[:, q:q + HALF], idx[:, bass.ds(n * NB + q, HALF)]).then_inc(Z["staged"], 1)
                            pool.wait_ge(Z["staged"], m + 1)
                            pool.sem_inc(Z["turn"])
                            for b in range(HALF):
                                if b:
                                    pool.wait_ge(Z["buf_free"], HALF * m + b + 1)
                                    pool.sem_inc(Z["turn"])
                                nc.gpsimd.indirect_dma_start(
                                    out=gbuf[:, q + b, :], out_offset=None, in_=I["peer_uv"],
                                    in_offset=bass.IndirectOffsetOnAxis(ap=estage[:, q + b:q + b + 1], axis=0)).then_inc(gath[q + b], 16)
                if g.latent:
                    with pool.Fori(1, TILES) as t:
                        tile(t)
                else:
                    tile(0)

            with pool.Fori(0, DEPTH) as l:
                for g in GR:
                    if g.latent:
                        meet(pool, 2 * l + 1)
                    dense(g)
                pool.wait_ge(GR[1].s["gw"], 4)
                pool.sem_inc(Z["buf_free"], NB)
                for g in GR:
                    experts(g)
                meet(pool, 2 * l + 2)


def constants():
    f = np.float32
    t = np.arange(DEC_SEQ, dtype=f)
    n_freq = ROPE // 4
    inv = (1.0 / (10000.0 ** (np.arange(n_freq, dtype=f) / n_freq))).astype(f)
    ang = np.concatenate([(t // GRID_W)[:, None] * inv, (t % GRID_W)[:, None] * inv], axis=1).astype(f)
    cos, sin = np.cos(ang), np.sin(ang)
    tab = np.stack([np.concatenate([cos, cos], 1), np.concatenate([-sin, sin], 1)])
    out = {"trig": tab.reshape(2, 4, 128, ROPE).transpose(2, 0, 1, 3).reshape(128, -1)}
    zs, nts = [], []
    for n in (SEQ, DEC_SEQ):
        tt = (np.arange(n, dtype=f) / f(n)).astype(f)
        a = (f(2.0 * math.pi) * tt[:, None] * np.arange(1, BANDS + 1, dtype=f)).astype(f)
        zs.append(np.concatenate([tt[:, None], np.sin(a), np.cos(a)], axis=1).T)
        nts.append(-tt.reshape(-1, 128).T)
    out["zT"] = np.concatenate(zs, axis=1)
    out["negt"] = np.concatenate(nts, axis=1)
    out["ident"] = np.eye(128)
    out["iota"] = np.tile(np.arange(NC), (128, 1))
    out["loff"] = np.stack([np.full((128, 1), l * N_EXPERTS) for l in range(DEPTH)])
    for name, n in (("dft_p", SEQ), ("dft_s", DEC_SEQ)):
        k, tt = np.arange(n)[None, :], np.arange(n)[:, None]
        w = np.pi * (2 * k + 1) / (2 * n)
        mats = [np.cos(w * tt), np.sin(w * tt), np.cos(w * (tt + 0.5)), np.sin(w * (tt + 0.5))]
        out[name] = np.stack(mats).reshape(4, n // 128, 128, n).transpose(0, 2, 1, 3)
    return {k: np.ascontiguousarray(v, dtype=f) for k, v in out.items()}


def packed(w, m):
    l, r, c = w.shape
    return w.reshape(l, r // 128, 128, c // m, m).transpose(0, 3, 2, 1, 4).reshape(l, c // m, 128, r // 128 * m)


def kernel(**inputs):
    from concourse import bacc
    from concourse.bass_utils import run_bass_kernel_spmd

    v = {k: np.asarray(a) for k, a in inputs.items()}
    fm = lambda a: a.reshape(DEPTH, -1, 128).transpose(0, 2, 1)
    arr = {
        "x": np.concatenate([v["x_prompt"][0], v["x_sample"][0]], axis=0),
        "cond": np.stack([v["c_ctx"], v["c"][0]]).reshape(2, KD, 128).transpose(2, 1, 0).reshape(128, 16),
        "w_ada": packed(v["w_ada"], 256), "w_qkv": packed(v["w_in"][:, :, :HY0], HY0), "w_hy": packed(v["w_in"][:, :, HY0:GT0], 256),
        "w_ga": packed(v["w_in"][:, :, GT0:GT0 + D], 256), "w_gb": packed(v["w_in"][:, :, GT0 + D:], 256),
        "w_uq": packed(v["w_uq"], 768), "w_ukv": packed(v["w_ukv"], 1024), "w_out": packed(v["w_out"], 256),
        "w_oab": packed(np.concatenate([v["w_oa"], v["w_ob"]], axis=1), 256), "w_wq": packed(v["peer_wq"], 256),
        "keysT": v["peer_keys"].reshape(DEPTH, NHP, NK, 128).transpose(0, 3, 1, 2).reshape(DEPTH, 128, NHP * NK),
        "lvec": np.concatenate([fm(v["b_ada"]), fm(v["norm_mix"]), fm(v["norm_ffn"])], axis=2),
        "q_norm": v["q_norm"], "kv_norm": v["kv_norm"],
        "cache_ckv": v["cache_ckv"][0], "cache_kr": v["cache_krope"][0],
        "convw": np.concatenate([v["hy_conv_w"], v["hy_conv_b"][:, None]], axis=1).reshape(DEPTH, 4, 12, 128)
            .transpose(0, 3, 2, 1).reshape(DEPTH, 128, 48),
        "hy_w1": v["hy_w1"], "hy_w2": v["hy_w2"], "hy_b": np.stack([v["hy_b1"], v["hy_b2"]], axis=2), "hy_w3": v["hy_w3"],
        "decay": v["hy_decay"].reshape(2 * DEPTH, 2 * HYW),
        "hy_bias": v["hy_bias"].reshape(DEPTH, 1, 2 * HYW),
        "peer_uv": np.concatenate([v["peer_u"], v["peer_v"]], axis=2).reshape(DEPTH * N_EXPERTS, 2 * D),
        "final_norm": v["final_norm"],
    }
    arr.update(constants())
    arr = {"in_" + k: np.ascontiguousarray(a) for k, a in arr.items()}
    nc = bacc.Bacc("TRN2", target_bir_lowering=False, num_devices=1)
    I = {k[3:]: nc.dram_tensor(k, a.shape, mybir.dt.from_np(a.dtype), kind="ExternalInput").ap()
         for k, a in arr.items()}
    O = {k: nc.dram_tensor("out_" + k, s, mybir.dt.float32, kind="ExternalOutput").ap()
                           for k, s in (("y", (SEQ + DEC_SEQ, D)), ("ckv", (DEPTH, 128, KVR)), ("kr", (DEPTH, 128, ROPE)))}
    build(nc, I, O)
    r = run_bass_kernel_spmd(nc, [arr], core_ids=[0]).results[0]
    y = r["out_y"]
    return (y[:SEQ].reshape(1, SEQ, D), y[SEQ:].reshape(1, DEC_SEQ, D),
            r["out_ckv"].reshape(1, DEPTH, SEQ, KVR), r["out_kr"].reshape(1, DEPTH, SEQ, ROPE))
```

```python
import math
from contextlib import ExitStack

import concourse.bass as bass
import numpy as np
from concourse import mybir

D, KD = 1024, 8
DEPTH, SEQ, DEC_SEQ, PAST, GRID_W = 2, 128, 512, 128, 64
NH, NOPE, ROPE, VD, QR, KVR = 8, 64, 32, 64, 384, 256
HQ = NOPE + ROPE
HYW, HID, EMB, BANDS = 512, 64, 33, 16
PH, NK, TOPK = 8, 128, 16
NHP = 2 * PH
N_EXPERTS = NK * NK
IN_COLS = QR + KVR + ROPE + 3 * HYW + 2 * D
HY0, GT0 = QR + KVR + ROPE, QR + KVR + ROPE + 3 * HYW
EPS = 1e-6
TILES = (SEQ + DEC_SEQ) // 128
SLOTS = PH * TOPK
NB = 8
HALF = NB // 2
ITERS = SLOTS // NB
WIDTHS = [TOPK // (i + 1) for i in range(TOPK)]
NC = sum(WIDTHS)
RUNS = [(0, 1, 16), (1, 1, 8), (2, 1, 5), (3, 1, 4), (4, 1, 3), (5, 3, 2), (8, 8, 1)]
MAGIC = 12582912.0
TWO_PI_HI = 6.28125
TWO_PI_LO = 2.0 * math.pi - TWO_PI_HI
GELU_A, GELU_C = 0.044715, math.sqrt(2.0 / math.pi)
SLOT_W = 2048


class Group:

    def __init__(self, name):
        self.name, self.latent = name, name == "s"
        self.t0, self.nt, self.nk, self.gi = (1, 4, 5, 1) if self.latent else (0, 1, 1, 0)
        self.T, self.TK = self.nt * 128, self.nk * 128
        self.ckv_banks = -(-2 * self.nk // 4)
        self.kr_banks = -(-self.nk // 4)
        self.k_pieces = ([(h, 1, 0, 4) for h in range(NH)] if self.latent else []) + \
            [(h, 4, self.nk - 1, 1) for h in (0, 4)]
        self.s = {}


def weight_loads(groups):
    loads = [(("ada", i), 1, (None, "ada_ps", i + 1)) for i in range(24)]
    for g in groups:
        n = g.name
        loads.append(((n, "qkv"), 3, (n, "qkv_ps", 2 * g.nt)))
        loads.append(((n, "ukv"), 1, (n, "v_ps", g.nk)))
        loads.append(((n, "uq"), 2, (n, "q_ps", g.nt)))
        loads += [((n, "hy", i), 1, (n, "hyc_ps", 2 * i + 2)) for i in range(6)]
        loads += [((n, "C"), 1, (n, "K_ps", 4 * g.nt)), ((n, "S"), 1, (n, "K_ps", 4 * g.nt)),
                  ((n, "Mc"), 1, (n, "y_ps", 8)), ((n, "Ms"), 1, (n, "y_ps", 8))]
        for i in range(4):
            c = 4 * 2 * (i + 1)
            loads += [((n, "ga", i), 1, (n, "mg_ps", c)), ((n, "gb", i), 1, (n, "mg_ps", c)),
                      ((n, "oab", i), 1, (n, "mg_ps", c))]
        loads += [((n, "out", i), 1, (n, "out_ps", 4 * (g.nt - 1) + i + 1)) for i in range(4)]
        loads += [((n, "keys"), 1, (n, "sc_ps", NHP))]
        loads += [((n, "wq", i), 1, (n, "qh_ps", 2 * i + 2)) for i in range(8)]
    placed, at, held = {}, 0, None
    for name, k, free in loads:
        if name[-1] == "keys":
            placed[name] = (3, 1, free)
            at, held = 0, 3
            continue
        if held is not None and name[1] != "wq":
            at, held = 0, None
        ring = 3 if held is not None else 4
        if at + k > ring:
            at = 0
        placed[name] = (at, k, free)
        at = (at + k) % ring
    return placed


GROUP_SEMS = """ss1 xn tr1 hT1 qkv_ps qkv_raw ss_qkv cn trc cT q_ps q_tm q_rope trq qT k_ps kT v_ps v
 s_ps smax prob trp pT o_ps attn tra aT hyc_ps hyc_mid hyc f_ps f_red f h_ps win wh sd K_ps K
 tru u U_ps Ym Yc y_ps y mg_ps th mm mg dgr bias0 row_ps row out_ps r2 xadd ss2 h2 tr2 hT2
 qh_ps qh sc_ps sc top ge gw ctx state arrived""".split()
SHARED_SEMS = """sc_saved sc_back ada_ps arow ada_tr mod chain pchain slot0 slot1 slot2 slot3 lvec lrow lfil ldec0 ldec1 lw3a lw3b
 buf_free staged turn ttr p_small inner th_e w_ready diag acc_read h2c""".split()


def build(nc, I, O):
    f32, u32, i32 = mybir.dt.float32, mybir.dt.uint32, mybir.dt.int32
    ALU, ACT, AX = mybir.AluOpType, mybir.ActivationFunctionType, mybir.AxisListType
    GR = [Group("p"), Group("s")]
    LOADS = weight_loads(GR)
    ctx = ExitStack()
    with ctx:
        def sb(name, words, dt=f32, parts=128):
            return ctx.enter_context(nc.sbuf_tensor("sb_" + name, [parts, words], dt))

        xflat = sb("x", TILES * D)
        x = xflat[:, :].rearrange("p (t d) -> p t d", d=D)
        hT = sb("hT", KD * 512)
        g2 = sb("g2", 2 * D)[:, :].rearrange("p (g d) -> p g d", g=2)
        slots = sb("slots", 4 * SLOT_W)
        keep = sb("keep", 4096)
        h2p = sb("h2p", D)
        arena = sb("arena", 22400)
        idx = sb("idx", TILES * SLOTS, u32)
        gwt = sb("gwt", TILES * SLOTS)
        ident, ones, zeros = sb("ident", 128), sb("ones", 128), sb("zeros", 128)
        cfm, cth = sb("cfm", 16), sb("cth", 16)
        mod = sb("mod", 96)[:, :].rearrange("p (c g) -> p c g", g=2)
        fold = sb("fold", 48)[:, :].rearrange("p (v c g) -> p v c g", v=3, g=2)
        lvec = sb("lvec", 64)
        qn_row, kvn_row = sb("qn_row", QR), sb("kvn_row", KVR)
        krp = sb("krp", 5 * HQ)[:, :].rearrange("p (k c) -> p k c", c=HQ)
        trig = sb("trig", 2 * 4 * ROPE)[:, :].rearrange("p (v j c) -> p v j c", v=2, j=4)
        negt = sb("negt", TILES)
        loff = sb("loff", 1)
        convw = sb("convw", 48)[:, :].rearrange("p (m v) -> p m v", v=4)
        fw1, fw2, fb = sb("fw1", HID, parts=EMB), sb("fw2", HID, parts=HID), sb("fb", 2, parts=HID)
        zT = sb("zT", SEQ + DEC_SEQ, parts=EMB)
        hyb = sb("hyb", 2 * HYW, parts=1)
        iota = sb("iota", NC)
        st = sb("st", 64)
        ssum = sb("ssum", 64)
        nmax = sb("nmax", 4)

        ps = ctx.enter_context(nc.psum_tensor("ps", [128, 8, 512], f32))
        psf = ps[:, :, :].rearrange("p b n -> p (b n)")

        def sem(name):
            return ctx.enter_context(nc.semaphore("k_" + name))

        setup, silu, out_done, final, fch, go = (sem(n) for n in ("setup", "silu", "out_done", "final", "fch", "go"))
        passed, final_sq = sem("passed"), sem("final_sq")
        Z = {n: sem(n) for n in SHARED_SEMS}
        nums = [v.num for v in Z.values()]
        gath = [sem(f"gath{b}") for b in range(NB)]
        of_group = {n: sem("g_" + n) for n in GROUP_SEMS}
        GR[0].s = GR[1].s = of_group
        group_nums = [v.num for v in of_group.values()]
        for part in (nums, group_nums):
            assert part == list(range(part[0], part[0] + len(part)))
        slot_full = [Z["slot0"], Z["slot1"], Z["slot2"], Z["slot3"]]

        def a(at, words):
            return arena[:, at:at + words]

        def a3(at, n, m):
            return arena[:, at:at + n * m].rearrange("p (n m) -> p n m", m=m)

        xn = a3(0, 4, D)
        xn2 = a3(8192, 4, D)
        cqraw, kvraw, cqn = a3(0, 4, QR), a3(1536, 4, 288), a3(2688, 4, QR)
        prob, probT, attn_all = a3(0, 2, 640), a3(1280, 2, 640), a3(2560, 4, 512)
        ckvn = a3(4224, 5, KVR)
        cqnT, ckvT = a3(5504, 3, 512), a(7040, 1280)
        q_tm = a3(8320, 2, 768)
        rope_tmp = a(9856, 768)
        qT, KT, V = a3(10624, 8, 512), a(14720, 5120), a3(19840, 5, 512)
        junk = a(21376, 1024)
        arow = arena[0:2, 20352:21376].rearrange("p (i n) -> p i n", i=4)
        hyT = a3(0, 12, 512)
        Kf = a(6144, 4096).rearrange("p (r k n) -> p r k n", r=2, k=4)
        Yf = a(10240, 4096).rearrange("p (r k n) -> p r k n", r=2, k=4)
        u_tm = a3(14336, 4, 512)
        w3 = arena[0:HID, 14336:14336 + 2048]
        decay = a3(16384, 2, 512)
        win, wh = a3(17408, 2, 512), a3(18432, 4, 512)
        prodm = a(17408, 4096).rearrange("p (b v n) -> p b v n", b=2, v=4)
        ftmp = a3(20480, 3, 512)
        f1T, f2T = arena[0:HID, 6144:6656], arena[0:HID, 21504:22016]
        mergedT = a3(0, 8, 512)
        tg, mtmp = a3(4096, 4, 512), a3(6144, 4, 512)
        rows = a3(12288, 3, D)
        dgr = a3(15360, 8, 128)
        otmp = a3(16384, 2, 256)
        scores = a(0, 8192).rearrange("p (j h n) -> p j h n", j=4, h=NHP)
        scores_p = a3(17408, NHP, NK)
        qh = a3(12288, 4, 512)

        def routing_memory(scr, at):
            v = {"scr": a3(scr, NHP, NK), "s16": a3(at, NHP, 16), "i16": a3(at + 256, NHP, 16), "i16f": a3(at + 512, NHP, 16),
                 "expert": a3(at + 512, PH, 16),
                 "cand": a3(at + 768, PH, NC), "cidx": a3(at + 1168, PH, NC), "scr2": a3(at + 1568, PH, NC),
                 "eq": a(at + 2048, 3200).rearrange("p (h k c) -> p h k c", h=PH // 2, k=16), "top": a3(at + 5248, PH, 16),
                 "pos": a3(at + 5376, PH, 16), "posf": a3(at + 5504, PH, 16), "gex": a3(at + 5632, PH, 16), "gsum": a(at + 5760, 8)}
            return v

        routing_s, routing_p = routing_memory(8192, 10240), routing_memory(10240, 15360)
        scores_back = a3(8192, NHP, NK)
        dge = a3(16128, NB, 128)
        dots, dsq, din, dth, dw = (a(17152 + 8 * i, 8) for i in range(5))
        estage = a(17192, NB).bitcast(u32)
        eacc = a(17200, D)
        gbuf = [slots[:, i * 2 * D:(i + 1) * 2 * D] for i in range(4)] + \
            [hT[:, i * 2 * D:(i + 1) * 2 * D] for i in range(2)] + [a(18304 + i * 2 * D, 2 * D) for i in range(2)]
        h2c = a(0, D)
        attnT, hyoT = (keep[:, i * 2048:(i + 1) * 2048].rearrange("p (c t) -> p c t", t=512) for i in (0, 1))
        h2s = keep[:, :].rearrange("p (j d) -> p j d", d=D)
        hT3 = hT[:, :].rearrange("p (k t) -> p k t", t=512)

        def slot_of(name, words=SLOT_W):
            s0, k, _ = LOADS[name]
            return slots[:, s0 * SLOT_W:s0 * SLOT_W + words]

        def h2_of(g, j):
            return h2s[:, j, :] if g.latent else h2p[:, :]

        def KTv(g):
            return KT[:, 0:NH * g.TK].rearrange("p (h t) -> p h t", h=NH)

        def signal(gname, s):
            if gname is None:
                return Z[s]
            return of_group[s]

        saved_scores = nc.dram_tensor("saved_scores", (128, NHP * NK), f32, kind="Internal").ap()
        block = ctx.enter_context(nc.Block())

        def beside(g, i):
            return range((i - 2) * 2 * g.nt // 4, (i - 1) * 2 * g.nt // 4)

        def meet(eng, count):
            eng.drain().then_inc(of_group["arrived"], 1)
            eng.wait_ge(go, count)
            eng.sem_inc(passed)

        @block.sync
        def _(sp):
            sp.dma_start(x, I["x"].rearrange("(t p) d -> p t d", p=128)).then_inc(setup, 16)
            for dst, src in ((cfm, I["cond"]), (trig.rearrange("p v j c -> p (v j c)"), I["trig"]), (negt, I["negt"]),
                             (zT, I["zT"]), (ident, I["ident"]), (iota, I["iota"])):
                sp.dma_start(dst[:, :], src).then_inc(setup, 16)

            def source(name, l):
                kind = name[1] if name[0] in ("p", "s") else name[0]
                g = GR[1 if name[0] == "s" else 0]

                packed = {"ada": 256, "hy": 256, "ga": 256, "gb": 256, "oab": 256, "out": 256, "wq": 256, "qkv": HY0, "ukv": 1024, "uq": 768}
                if kind in packed:
                    w, m = I["w_" + kind], packed[kind]
                    n = w.shape[-1] // m
                    i = name[-1] if kind not in ("qkv", "ukv", "uq") else 0
                    return w[bass.ds(l, 1), i].rearrange("o p (n m) -> p (o n) m", m=m), (n, m)
                if kind == "keys":
                    return I["keysT"][bass.ds(l, 1)].rearrange("o p (h n) -> p (o h) n", h=NHP), (NHP, NK)
                src = {"C": 0, "S": 1, "Mc": 2, "Ms": 3}[kind]
                if g.latent:
                    return I["dft_s"][src], (4, 512)
                return I["dft_p"][src], (1, 128)

            with sp.Fori(0, DEPTH) as l:
                sp.dma_start(lvec[:, :], I["lvec"][bass.ds(l, 1)].rearrange("o p n -> p (o n)")).then_inc(Z["lvec"], 16)
                for dst, src in ((qn_row, I["q_norm"]), (kvn_row, I["kv_norm"])):
                    sp.dma_start(dst[:, :], src[bass.ds(l, 1), :].rearrange("o n -> (o n)").partition_broadcast(128)).then_inc(Z["lrow"], 16)
                sp.dma_start(loff[:, :], I["loff"][bass.ds(l, 1)].rearrange("o p n -> p (o n)")).then_inc(Z["lrow"], 16)
                sp.dma_start(convw, I["convw"][bass.ds(l, 1)].rearrange("o p (m v) -> p (o m) v", v=4)).then_inc(Z["lrow"], 16)
                for dst, src in ((fw1, I["hy_w1"]), (fw2, I["hy_w2"]), (fb, I["hy_b"]), (hyb, I["hy_bias"])):
                    sp.dma_start(dst[:, :], src[bass.ds(l, 1)].rearrange("o p n -> p (o n)")).then_inc(Z["lfil"], 16)
                last = {}
                for name, (s0, k, free) in LOADS.items():
                    g = GR[1 if name[0] == "s" else 0]
                    for s in range(s0, s0 + k):
                        if s in last:
                            sp.wait_ge(signal(last[s][0], last[s][1]), last[s][2])
                        last[s] = free
                    src, (n, m) = source(name, l)
                    sp.dma_start(slots[:, s0 * SLOT_W:s0 * SLOT_W + n * m].rearrange("p (n m) -> p n m", m=m),
                                 src).then_inc(slot_full[s0], 16)
                    if name[0] == "s" and name[1] == "ukv":
                        sp.wait_ge(of_group["sc"], NHP)
                        sp.dma_start(saved_scores, scores_p.rearrange("p h n -> p (h n)")).then_inc(Z["sc_saved"], 16)
                        sp.wait_ge(of_group["arrived"], 4)
                        sp.sem_clear(range(group_nums[0], group_nums[-1] + 1))
                        sp.sem_inc(go)
                        last = {q: v for q, v in last.items() if v[0] == "s"}
                        sp.dma_start(ckvn[:, 0, :], I["cache_ckv"][bass.ds(l, 1)].rearrange("o p n -> p (o n)")).then_inc(g.s["ctx"], 16)
                        sp.dma_start(krp[:, 0, NOPE:HQ], I["cache_kr"][bass.ds(l, 1)].rearrange("o p n -> p (o n)")).then_inc(g.s["ctx"], 16)
                    if name == ("s", "oab", 0):
                        sp.wait_ge(Z["sc_saved"], 16)
                        sp.wait_ge(g.s["y_ps"], 8)
                        sp.dma_start(scores_back.rearrange("p h n -> p (h n)"), saved_scores).then_inc(Z["sc_back"], 16)
                    if name[0] in ("p", "s") and name[1] == "uq" and not g.latent:
                        sp.wait_ge(g.s["cn"], 1)
                        sp.dma_start(O["ckv"][bass.ds(l, 1)].rearrange("o p n -> p (o n)"), ckvn[:, 0, :]).then_inc(g.s["state"], 16)
                        sp.dma_start(O["kr"][bass.ds(l, 1)].rearrange("o p n -> p (o n)"), krp[:, 0, NOPE:HQ]).then_inc(g.s["state"], 16)
                    if name[0] in ("p", "s") and name[1] == "hy" and name[2] == 3:
                        sp.wait_ge(g.s["attn"], g.nt)
                        sp.wait_ge(g.s["tra"], g.nt)
                        if not g.latent:
                            sp.wait_ge(g.s["state"], 32)
                        sp.dma_start(w3, I["hy_w3"][bass.ds(l, 1)].rearrange("o p n -> p (o n)")).then_inc(Z["lw3a"], 16)
                        sp.dma_start(arena[:, 16384:17408], I["decay"][bass.ds(2 * l, 1)].rearrange("o n -> (o n)").partition_broadcast(128)).then_inc(Z["ldec0"], 16)
                    if name[0] in ("p", "s") and name[1] == "Ms":
                        sp.wait_ge(g.s["win"], 2 * g.nt)
                        sp.dma_start(arena[:, 16384:17408], I["decay"][bass.ds(2 * l + 1, 1)].rearrange("o n -> (o n)").partition_broadcast(128)).then_inc(Z["ldec1"], 16)
                        sp.wait_ge(g.s["U_ps"], g.nt)
                        sp.dma_start(w3, I["hy_w3"][bass.ds(l, 1)].rearrange("o p n -> p (o n)")).then_inc(Z["lw3b"], 16)
                sp.wait_ge(of_group["arrived"], 4)
                sp.sem_clear(range(group_nums[0], group_nums[-1] + 1))
                sp.sem_clear(range(nums[0], nums[-1] + 1))
                sp.sem_inc(go)
            sp.dma_start(arena[:, 0:D], I["final_norm"].partition_broadcast(128)).then_inc(final, 16)
            sp.wait_ge(fch, 1)
            sp.dma_start(O["y"].rearrange("(t p) d -> p t d", p=128), x).then_inc(out_done, 16)
            sp.wait_ge(out_done, 16)

        @block.tensor
        def _(pe):
            busy, used = {}, {}

            def claim(bank, s, value):
                if bank in busy:
                    pe.wait_ge(*busy[bank])
                busy[bank] = (s, value)

            def loaded(name):
                s0, k, _ = LOADS[name]
                order = [n for n in LOADS if LOADS[n][0] == s0]
                pe.wait_ge(slot_full[s0], 16 * (order.index(name) + 1))

            def w3d(name, m, n=8):
                return slot_of(name, n * m).rearrange("p (n m) -> p n m", m=m)

            def adaln():
                claim(7, Z["mod"], 1)
                pe.wait_ge(silu, 4)
                for i in range(25):
                    if i < 24:
                        loaded(("ada", i))
                        w = w3d(("ada", i), 256)
                        claim(4 + i % 3, Z["arow"], i + 1)
                        for k in range(KD):
                            m = pe.matmul(ps[0:2, 4 + i % 3, 0:256], cfm[:, 2 * k:2 * k + 2], w[:, k, :], start=(k == 0), stop=(k == 7))
                        m.then_inc(Z["ada_ps"], 1)
                    if i >= 1:
                        pe.wait_ge(Z["arow"], i)
                        for c in (0, 1):
                            at = 4 * (i - 1) + 2 * c
                            m = pe.transpose(ps[:, 7, at:at + 2], arow[:, (i - 1) % 4, c * 128:c * 128 + 128], ident[0:2, 0:2])
                        m.then_inc(Z["ada_tr"], 1)

            def dense(g):
                s, nt, T = g.s, g.nt, g.T
                n = g.name
                pe.wait_ge(setup, 16 * 7)
                pe.wait_ge(s["xn"], nt)
                for c in range(KD):
                    claim(c % 4, s["hT1"], c + 1)
                    for j in range(nt):
                        m = pe.transpose(ps[:, c % 4, j * 128:j * 128 + 128], xn[:, j, c * 128:c * 128 + 128], ident[:, :])
                    m.then_inc(s["tr1"], 1)
                loaded((n, "qkv"))
                w = w3d((n, "qkv"), HY0)
                pe.wait_ge(s["hT1"], KD)
                for j in range(nt):
                    for v, (c0, cn) in enumerate(((0, QR), (QR, KVR + ROPE))):
                        b = (2 * j + v) % 4
                        claim(b, s["ss_qkv"], 2 * j + v + 1)
                        for k in range(KD):
                            m = pe.matmul(ps[:, b, 0:cn], hT3[:, k, j * 128:j * 128 + 128], w[:, k, c0:c0 + cn],
                                          start=(k == 0), stop=(k == 7))
                        m.then_inc(s["qkv_ps"], 1)
                pe.wait_ge(s["cn"], nt)
                if g.latent:
                    pe.wait_ge(s["ctx"], 32)
                at = 0
                for c in range(3):
                    claim(4 + at % 4, s["cT"], at + 1)
                    for j in range(nt):
                        m = pe.transpose(ps[:, 4 + at % 4, j * 128:j * 128 + 128], cqn[:, j, c * 128:c * 128 + 128], ident[:, :])
                    m.then_inc(s["trc"], 1)
                    at += 1
                for q in range(g.ckv_banks):
                    claim(4 + at % 4, s["cT"], at + 1)
                    for r in range(4 * q, min(4 * q + 4, 2 * g.nk)):
                        m = pe.transpose(ps[:, 4 + at % 4, (r % 4) * 128:(r % 4) * 128 + 128],
                                         ckvn[:, r % g.nk, (r // g.nk) * 128:(r // g.nk) * 128 + 128], ident[:, :])
                    m.then_inc(s["trc"], 1)
                    at += 1
                for q in range(g.kr_banks):
                    claim(4 + at % 4, s["cT"], at + 1)
                    for r in range(4 * q, min(4 * q + 4, g.nk)):
                        m = pe.transpose(ps[0:HQ, 4 + at % 4, (r % 4) * 128:(r % 4) * 128 + 128], krp[:, r, :], ident[:, :])
                    m.then_inc(s["trc"], 1)
                    at += 1
                loaded((n, "uq"))
                w = w3d((n, "uq"), 768, 3)
                pe.wait_ge(s["cT"], 3)

                def q_proj(j):
                    for v in (0, 1):
                        b = 2 * (j % 2) + v
                        claim(b, s["q_tm"], j + 1)
                        for k in range(3):
                            m = pe.matmul(ps[:, b, 0:QR], cqnT[:, k, j * 128:j * 128 + 128], w[:, k, v * QR:v * QR + QR],
                                          start=(k == 0), stop=(k == 2))
                    m.then_inc(s["q_ps"], 1)

                def q_turn(j):
                    pe.wait_ge(s["q_rope"] if g.latent else s["q_tm"], j + 1)
                    for v in (0, 1):
                        b = 4 + (2 * j + v) % 4
                        claim(b, s["qT"], 2 * j + v + 1)
                        for h in range(4):
                            m = pe.transpose(ps[0:HQ, b, h * 128:h * 128 + 128],
                                             q_tm[:, j % 2, (4 * v + h) * HQ:(4 * v + h + 1) * HQ], ident[:, :])
                        m.then_inc(s["trq"], 1)

                for j in range(nt + 1):
                    if j < nt:
                        q_proj(j)
                    if j >= 1:
                        q_turn(j - 1)
                loaded((n, "ukv"))
                w = w3d((n, "ukv"), 1024, 2)
                pe.wait_ge(s["cT"], 3 + g.ckv_banks)
                ck = ckvT[:, 0:2 * g.TK].rearrange("p (c t) -> p c t", c=2)
                for i, (h0, nh, kt, n_kt) in enumerate(g.k_pieces):
                    b = i % 4
                    claim(b, s["kT"], i + 1)
                    for h in range(nh):
                        for k in (0, 1):
                            m = pe.matmul(ps[0:NOPE, b, h * 128:h * 128 + n_kt * 128], w[:, k, (h0 + h) * 128:(h0 + h) * 128 + NOPE],
                                          ck[:, k, kt * 128:(kt + n_kt) * 128], start=(k == 0), stop=(k == 1))
                    m.then_inc(s["k_ps"], 1)
                for kt in range(g.nk):
                    b = 4 + kt % 4
                    claim(b, s["v"], kt + 1)
                    for k in (0, 1):
                        wv = w[:, k, :].rearrange("p (h c) -> p h c", h=NH)[:, :, NOPE:NOPE + VD]
                        m = pe.matmul(ps[:, b, :].rearrange("p (h c) -> p h c", h=NH), ck[:, k, kt * 128:kt * 128 + 128], wv,
                                      start=(k == 0), stop=(k == 1))
                    m.then_inc(s["v_ps"], 1)
                pe.wait_ge(s["qT"], 2 * nt)
                pe.wait_ge(s["kT"], len(g.k_pieces))
                pe.wait_ge(s["cT"], 3 + g.ckv_banks + g.kr_banks)
                pe.wait_ge(s["v"], g.nk)
                kv, N = KTv(g), nt * NH
                for b in range(8):
                    if b in busy:
                        pe.wait_ge(*busy.pop(b))
                for i in range(N + 2):
                    if i < N:
                        j, h, b = i // NH, i % NH, 2 * (i % 2)
                        claim(b, s["prob"], i + 1)
                        for c0 in range(0, g.TK, 512):
                            cn = min(512, g.TK - c0)
                            m = pe.matmul(psf[:, b * 512 + c0:b * 512 + c0 + cn], qT[0:HQ, h, j * 128:j * 128 + 128],
                                          kv[0:HQ, h, c0:c0 + cn], start=True, stop=True)
                        m.then_inc(s["s_ps"], 1)
                    if 1 <= i <= N:
                        pe.wait_ge(s["prob"], i)
                        claim(4, s["pT"], i)
                        for kt in range(g.nk):
                            m = pe.transpose(psf[:, 4 * 512 + kt * 128:4 * 512 + kt * 128 + 128],
                                             prob[:, (i - 1) % 2, kt * 128:kt * 128 + 128], ident[:, :])
                        m.then_inc(s["trp"], 1)
                    if i >= 2:
                        j, h = (i - 2) // NH, (i - 2) % NH
                        b = 6 + j % 2
                        if h == 0:
                            claim(b, s["attn"], j + 1)
                        pe.wait_ge(s["pT"], i - 1)
                        for kt in range(g.nk):
                            m = pe.matmul(ps[:, b, h * VD:h * VD + VD], probT[:, i % 2, kt * 128:kt * 128 + 128],
                                          V[:, kt, h * VD:h * VD + VD], start=(kt == 0), stop=(kt == g.nk - 1))
                        m.then_inc(s["o_ps"], 1)
                for b in (0, 2, 4, 6, 7):
                    if b in busy:
                        pe.wait_ge(*busy.pop(b))
                for j in range(nt):
                    claim(j % 4, s["aT"], j + 1)
                    pe.wait_ge(s["attn"], j + 1)
                    for c in range(4):
                        m = pe.transpose(ps[:, j % 4, c * 128:c * 128 + 128], attn_all[:, j, c * 128:c * 128 + 128], ident[:, :])
                    m.then_inc(s["tra"], 1)
                z0 = 0 if not g.latent else SEQ

                def filters(o, part):
                    pe.wait_ge(Z["lw3b"] if o else Z["lw3a"], 16 * (g.gi + 1))
                    for i in part:
                        i += o * 2 * nt
                        claim(i % 4, s["wh"], i + 1)
                        tc = (i // 2) % nt
                        pe.matmul(ps[:, i % 4, :], f2T[:, tc * 128:tc * 128 + 128], w3[:, (2 * o + i % 2) * HYW:(2 * o + i % 2 + 1) * HYW],
                                  start=True, stop=True).then_inc(s["h_ps"], 1)

                for i in range(6):
                    loaded((n, "hy", i))
                    w = w3d((n, "hy", i), 256)
                    for c in (0, 1):
                        mi = 2 * i + c
                        b = 4 + mi % 4
                        claim(b, s["hyc"], mi + 1)
                        for k in range(KD):
                            m = pe.matmul(ps[:, b, 0:T], w[:, k, c * 128:c * 128 + 128], hT3[:, k, 0:T], start=(k == 0), stop=(k == 7))
                        m.then_inc(s["hyc_ps"], 1)
                    if i == 0:
                        pe.wait_ge(Z["lfil"], 64)
                        claim(0, s["f_red"], 1)
                        pe.matmul(ps[0:HID, 0, 0:T], fw1[:, :], zT[:, z0:z0 + T], start=True, stop=True).then_inc(s["f_ps"], 1)
                    if i == 1:
                        pe.wait_ge(s["f"], 1)
                        claim(1, s["f_red"], 2)
                        pe.matmul(ps[0:HID, 1, 0:T], fw2[:, :], f1T[:, 0:T], start=True, stop=True).then_inc(s["f_ps"], 1)
                    if i >= 2:
                        pe.wait_ge(s["f"], 2)
                        filters(0, beside(g, i))

                def spectra(o):
                    if o:
                        filters(1, range(2 * nt))
                    pe.wait_ge(s["sd"], (o + 1) * nt)
                    for r, kind in enumerate(("C", "S")):
                        loaded((n, kind))
                        w = w3d((n, kind), T, nt)
                        for kc in range(nt):
                            i = (o * 2 + r) * nt + kc
                            claim(4 + i % 4, s["K"], i + 1)
                            for tc in range(nt):
                                m = pe.matmul(ps[:, 4 + i % 4, :], w[:, tc, kc * 128:kc * 128 + 128], Yf[:, r, tc, :],
                                              start=(tc == 0), stop=(tc == nt - 1))
                            m.then_inc(s["K_ps"], 1)

                def convolve(o):
                    pe.wait_ge(*((s["y"], 4) if o else (s["hyc"], 12)))
                    for j in range(nt):
                        claim(j % 4, s["u"], o * nt + j + 1)
                        for c in range(4):
                            m = pe.transpose(ps[:, j % 4, c * 128:c * 128 + 128], hyT[:, c, j * 128:j * 128 + 128], ident[:, :])
                        m.then_inc(s["tru"], 1)
                    pe.wait_ge(s["u"], (o + 1) * nt)
                    loaded((n, "Mc"))
                    loaded((n, "Ms"))
                    M = [w3d((n, kind), T, nt) for kind in ("Mc", "Ms")]
                    for kc in range(nt):
                        for r in (0, 1):
                            b = 4 + 2 * (kc % 2) + r
                            claim(b, s["Ym"], o * nt + kc + 1)
                            for tc in range(nt):
                                m = pe.matmul(ps[:, b, :], M[r][:, tc, kc * 128:kc * 128 + 128], u_tm[:, tc, :],
                                              start=(tc == 0), stop=(tc == nt - 1))
                        m.then_inc(s["U_ps"], 1)
                    pe.wait_ge(s["Yc"], (o + 1) * nt)
                    for c in range(4):
                        claim(c, s["y"], o * 4 + c + 1)
                        for r in (0, 1):
                            for kc in range(nt):
                                m = pe.matmul(ps[:, c, 0:T], Yf[:, r, kc, c * 128:c * 128 + 128], M[r][:, kc, 0:T],
                                              start=(r == 0 and kc == 0), stop=(r == 1 and kc == nt - 1))
                        m.then_inc(s["y_ps"], 1)

                for o in (0, 1):
                    spectra(o)
                    convolve(o)
                pe.wait_ge(s["aT"], nt)
                for c in range(KD):
                    i, cc = c // 2, (c % 2) * 128
                    for v, kind in enumerate(("ga", "gb", "oa", "ob")):
                        b = 4 * (c % 2) + v
                        claim(b, *((s["th"], 2 * c + v + 1) if v < 2 else (s["mm"], c + 1)))
                        if c == 0 and v == 3:
                            pe.wait_ge(s["y"], 8)
                        name = (n, kind if v < 2 else "oab", i)
                        loaded(name)
                        w = w3d(name, 256)
                        ks = range(KD) if v < 2 else range(4)
                        for k in ks:
                            if v < 2:
                                lhs, rhs = w[:, k, cc:cc + 128], hT3[:, k, 0:T]
                            else:
                                lhs, rhs = w[:, 4 * (v - 2) + k, cc:cc + 128], (attnT, hyoT)[v - 2][:, k, 0:T]
                            m = pe.matmul(ps[:, b, 0:T], lhs, rhs, start=(k == ks[0]), stop=(k == ks[-1]))
                        m.then_inc(s["mg_ps"], 1)
                    if c < 4:
                        pe.wait_ge(s["dgr"], c + 1)
                        for v in (0, 1):
                            b = 4 * ((c + 1) % 2) + v
                            claim(b, s["row"], 2 * c + v + 1)
                            pe.matmul(ps[:, b, :], ones[:, :], dgr[:, 4 * v:4 * v + 4, :].rearrange("p n m -> p (n m)"),
                                      start=True, stop=True).then_inc(s["row_ps"], 1)
                pe.wait_ge(s["mg"], KD)
                for q in range(4 * nt):
                    j, i = q // 4, q % 4
                    loaded((n, "out", i))
                    w = w3d((n, "out", i), 256)
                    claim(q % 8, s["r2"], q + 1)
                    for k in range(KD):
                        m = pe.matmul(ps[:, q % 8, 0:256], mergedT[:, k, j * 128:j * 128 + 128], w[:, k, :], start=(k == 0), stop=(k == 7))
                    m.then_inc(s["out_ps"], 1)
                pe.wait_ge(s["h2"], nt)
                for c in range(KD):
                    claim(c % 4, s["hT2"], c + 1)
                    for j in range(nt):
                        m = pe.transpose(ps[:, c % 4, j * 128:j * 128 + 128], h2_of(g, j)[:, c * 128:c * 128 + 128], ident[:, :])
                    m.then_inc(s["tr2"], 1)
                pe.wait_ge(s["hT2"], KD)
                for i in range(NHP + 1):
                    if i < NHP:
                        loaded((n, "wq", i // 2))
                        w = w3d((n, "wq", i // 2), 256)
                        b = 4 + i % 2
                        claim(b, s["qh"], i + 1)
                        for k in range(KD):
                            m = pe.matmul(ps[:, b, 0:T], w[:, k, (i % 2) * 128:(i % 2) * 128 + 128], hT3[:, k, 0:T], start=(k == 0), stop=(k == 7))
                        m.then_inc(s["qh_ps"], 1)
                    if i >= 1:
                        if i == 1:
                            loaded((n, "keys"))
                        kt = w3d((n, "keys"), NK, NHP)
                        pe.wait_ge(s["qh"], i)
                        b = 6 + (i - 1) % 2
                        claim(b, s["sc"], i)
                        for j in range(nt):
                            m = pe.matmul(ps[:, b, j * 128:j * 128 + 128], qh[:, (i - 1) % 4, j * 128:j * 128 + 128], kt[:, i - 1, :],
                                          start=True, stop=True)
                        m.then_inc(s["sc_ps"], 1)

            def experts(g):
                for b in (0, 1):
                    if b in busy:
                        pe.wait_ge(*busy.pop(b))
                n0 = g.t0 * ITERS

                def tile(t):
                    pe.wait_ge(Z["acc_read"], t + 1)
                    for c in (0, 1):
                        pe.matmul(ps[:, c, :], zeros[:, :], zeros[:, :].unsqueeze(1).to_broadcast([128, 4, 128]), start=True, stop=False, skip_group_check=True)
                    with pe.Fori(0, ITERS) as i:
                        for hf in (0, 1):
                            m4 = ((t * ITERS + i) * 2 + hf) * HALF
                            for b in range(HALF):
                                q = hf * HALF + b
                                pe.wait_ge(Z["diag"], m4 + b + 1)
                                for c in (0, 1):
                                    m = pe.matmul(ps[:, c, :], dge[:, q, :], gbuf[q][:, D + c * 512:D + c * 512 + 512],
                                                  start=False, stop=False, skip_group_check=True)
                                m.then_inc(Z["buf_free"], 1)
                if g.latent:
                    with pe.Fori(1, TILES) as t:
                        tile(t)
                else:
                    tile(0)

            with pe.Fori(0, DEPTH) as l:
                busy.clear()
                adaln()
                for g in GR:
                    if g.latent:
                        meet(pe, 2 * l + 1)
                        busy.clear()
                    dense(g)
                for g in GR:
                    experts(g)
                meet(pe, 2 * l + 2)

        @block.scalar
        def _(act):
            done = [0]

            act.wait_ge(setup, 16 * 7)
            act.activation(cth[:, :], cfm[:, :], ACT.Tanh, scale=0.5).then_inc(silu, 1)

            def dense(g):
                s, nt, T = g.s, g.nt, g.T
                for j in range(nt):
                    if j:
                        act.wait_ge(s["ss1"], j)
                    act.activation(junk, x[:, g.t0 + j, :], ACT.Square, accum_out=st[:, j:j + 1]).then_inc(s["ss1"], 1)
                act.wait_ge(Z["mod"], 4)
                for c in range(KD):
                    act.wait_ge(s["tr1"], c + 1)
                    act.activation(hT3[:, c, 0:T], ps[:, c % 4, 0:T], ACT.Identity, scale=fold[:, 0, c, g.gi:g.gi + 1],
                                   bias=mod[:, c, g.gi:g.gi + 1]).then_inc(s["hT1"], 1)
                for j in range(nt):
                    for v, (dst, w, sq) in enumerate(((cqraw, QR, QR), (kvraw, KVR + ROPE, KVR))):
                        i = 2 * j + v
                        act.wait_ge(s["qkv_ps"], i + 1)
                        act.activation(dst[:, j, 0:w], ps[:, i % 4, 0:w], ACT.Copy).then_inc(s["qkv_raw"], 1)
                        if i:
                            act.wait_ge(s["ss_qkv"], i)
                        act.activation(junk[:, 0:sq], ps[:, i % 4, 0:sq], ACT.Square, accum_out=st[:, 8 + v * nt + j:9 + v * nt + j]).then_inc(s["ss_qkv"], 1)
                at = 0
                for c in range(3):
                    act.wait_ge(s["trc"], at + 1)
                    act.activation(cqnT[:, c, 0:T], ps[:, 4 + at % 4, 0:T], ACT.Copy).then_inc(s["cT"], 1)
                    at += 1
                for q in range(g.ckv_banks):
                    w = (min(4 * q + 4, 2 * g.nk) - 4 * q) * 128
                    act.wait_ge(s["trc"], at + 1)
                    act.activation(ckvT[:, q * 512:q * 512 + w], ps[:, 4 + at % 4, 0:w], ACT.Copy).then_inc(s["cT"], 1)
                    at += 1
                if g.latent:
                    act.wait_ge(Z["sc_saved"], 16)
                for q in range(g.kr_banks):
                    w = (min(4 * q + 4, g.nk) - 4 * q) * 128
                    act.wait_ge(s["trc"], at + 1)
                    src = ps[NOPE:HQ, 4 + at % 4:5 + at % 4, 0:w].to_broadcast([ROPE, NH, w])
                    act.activation(KTv(g)[NOPE:HQ, :, q * 512:q * 512 + w], src, ACT.Copy).then_inc(s["cT"], 1)
                    at += 1
                for j in range(nt):
                    act.wait_ge(s["q_ps"], j + 1)
                    if j >= 2:
                        act.wait_ge(s["trq"], 2 * (j - 1))
                    b = 2 * (j % 2)
                    act.activation(q_tm[:, j % 2, :].rearrange("p (v c) -> p v c", v=2), ps[:, b:b + 2, 0:QR], ACT.Copy,
                                   scale=HQ ** -0.5).then_inc(s["q_tm"], 1)
                for kt in range(g.nk):
                    act.wait_ge(s["v_ps"], kt + 1)
                    act.activation(V[:, kt, :], ps[:, 4 + kt % 4, :], ACT.Copy).then_inc(s["v"], 1)
                for i in range(nt * NH):
                    act.wait_ge(s["smax"], i + 1)
                    if i >= 2:
                        act.wait_ge(s["trp"], i - 1)
                    b = 2 * (i % 2)
                    act.activation(prob[:, i % 2, 0:g.TK], psf[:, b * 512:b * 512 + g.TK], ACT.Exp, bias=nmax[:, i % 4:i % 4 + 1],
                                   accum_out=ssum[:, i:i + 1]).then_inc(s["prob"], 1)
                    if i >= 1:
                        turned(g, i - 1)
                turned(g, nt * NH - 1)
                for j in range(nt):
                    act.wait_ge(s["tra"], j + 1)
                    act.activation(attnT[:, :, j * 128:j * 128 + 128], ps[:, j % 4, :].rearrange("p (c t) -> p c t", c=4), ACT.Copy).then_inc(s["aT"], 1)
                act.wait_ge(Z["lrow"], 64)
                act.wait_ge(s["tra"], nt)
                if not g.latent:
                    act.wait_ge(s["state"], 32)
                def windows(o, part):
                    for i in part:
                        i += o * 2 * nt
                        tc = (i // 2) % nt
                        if i >= 2:
                            act.wait_ge(s["wh"], i - 1)
                        act.activation(win[:, i % 2, :], decay[:, i % 2, :], ACT.Exp, scale=negt[:, g.t0 + tc:g.t0 + tc + 1]).then_inc(s["win"], 1)

                for m in range(12):
                    act.wait_ge(s["hyc_ps"], m + 1)
                    act.activation(hyT[:, m, 0:T], ps[:, 4 + m % 4, 0:T], ACT.Identity, scale=convw[:, m, 1:2], bias=convw[:, m, 3:4]).then_inc(s["hyc_mid"], 1)
                    if m in (1, 3):
                        i = m // 2
                        act.wait_ge(s["f_red"], i + 1)
                        act.activation((f1T, f2T)[i][:, 0:T], ftmp[0:HID, 2, 0:T], ACT.Sin).then_inc(s["f"], 1)
                    if m == 5:
                        act.wait_ge(Z["ldec0"], 16 * (g.gi + 1))
                    if m >= 5 and m % 2:
                        windows(0, beside(g, m // 2))
                for o in (0, 1):
                    if o:
                        act.wait_ge(s["Yc"], nt)
                        act.wait_ge(Z["ldec1"], 16 * (g.gi + 1))
                        windows(1, range(2 * nt))
                    for i in range(2 * nt):
                        i += o * 2 * nt
                        act.wait_ge(s["K_ps"], i + 1)
                        act.activation(Kf[:, (i // nt) % 2, i % nt, :], ps[:, 4 + i % 4, :], ACT.Copy).then_inc(s["K"], 1)
                    for j in range(nt):
                        act.wait_ge(s["tru"], o * nt + j + 1)
                        act.activation(u_tm[:, j, :], ps[:, j % 4, :], ACT.Copy).then_inc(s["u"], 1)
                for c in range(KD):
                    for v in (0, 1):
                        act.wait_ge(s["mg_ps"], 4 * c + v + 1)
                        if c >= 2:
                            act.wait_ge(s["mm"], c - 1)
                        act.activation(tg[:, 2 * (c % 2) + v, 0:T], ps[:, 4 * (c % 2) + v, 0:T], ACT.Tanh, scale=0.5).then_inc(s["th"], 1)
                    if c < 4:
                        for v in (0, 1):
                            act.wait_ge(s["row_ps"], 2 * c + v + 1)
                            dst = rows[:, c, v * 512:v * 512 + 512] if c < 3 else g2[:, g.gi, v * 512:v * 512 + 512]
                            act.activation(dst, ps[:, 4 * ((c + 1) % 2) + v, :], ACT.Copy).then_inc(s["row"], 1)
                    if g.latent and c == 5:
                        gate_exp(0, routing_p["gex"])
                for j in range(nt):
                    act.wait_ge(s["xadd"], 4 * j + 4)
                    if j:
                        act.wait_ge(s["ss2"], j)
                    act.activation(junk, x[:, g.t0 + j, :], ACT.Square, accum_out=st[:, j:j + 1]).then_inc(s["ss2"], 1)
                for c in range(KD):
                    act.wait_ge(s["tr2"], c + 1)
                    act.activation(hT3[:, c, 0:T], ps[:, c % 4, 0:T], ACT.Copy).then_inc(s["hT2"], 1)
                for i in range(NHP):
                    act.wait_ge(s["qh_ps"], i + 1)
                    if i >= 4:
                        act.wait_ge(s["sc_ps"], i - 3)
                    act.activation(qh[:, i % 4, 0:T], ps[:, 4 + i % 2, 0:T], ACT.Copy).then_inc(s["qh"], 1)

            def gate_exp(t, gex):
                act.wait_ge(of_group["top"], t + 1)
                act.activation(gex, gex, ACT.Exp).then_inc(of_group["ge"], 1)

            def turned(g, i):
                act.wait_ge(g.s["trp"], i + 1)
                if i >= 2:
                    act.wait_ge(g.s["o_ps"], i - 1)
                act.activation(probT[:, i % 2, 0:g.TK], psf[:, 4 * 512:4 * 512 + g.TK], ACT.Copy).then_inc(g.s["pT"], 1)

            def experts(g):
                def iteration(n):
                    for hf in (0, 1):
                        m = n * 2 + hf
                        q = hf * HALF
                        act.wait_ge(Z["inner"], m + 1)
                        act.activation(dth[:, q:q + HALF], din[:, q:q + HALF], ACT.Tanh, scale=GELU_C).then_inc(Z["th_e"], 1)
                        act.wait_ge(Z["w_ready"], m + 1)
                        act.wait_ge(Z["buf_free"], HALF * (m + 1))
                        for b in range(HALF):
                            act.activation(dge[:, q + b, :], ident[:, :], ACT.Copy, scale=dw[:, q + b:q + b + 1]).then_inc(Z["diag"], 1)

                if g.latent:
                    with act.Fori(ITERS, TILES * ITERS) as n:
                        iteration(n)
                else:
                    with act.Fori(0, 4) as j:
                        for i in range(4):
                            iteration(j * 4 + i)
                            if i == 1:
                                gate_exp(j + 1, routing_s["gex"])

            with act.Fori(0, DEPTH) as l:
                for i in range(24):
                    act.wait_ge(Z["ada_ps"], i + 1)
                    if i >= 4:
                        act.wait_ge(Z["ada_tr"], i - 3)
                    act.activation(arow[:, i % 4, :], ps[0:2, 4 + i % 3, 0:256], ACT.Copy).then_inc(Z["arow"], 1)
                for g in GR:
                    if g.latent:
                        meet(act, 2 * l + 1)
                    dense(g)
                for g in GR:
                    experts(g)
                meet(act, 2 * l + 2)
            for j in range(TILES):
                if j:
                    act.wait_ge(final_sq, j)
                act.activation(junk, x[:, j, :], ACT.Square, accum_out=st[:, j:j + 1]).then_inc(final_sq, 1)

        @block.vector
        def _(dve):
            count = [0]

            def link(ins):
                count[0] += 1
                ins.then_inc(Z["chain"], 1)
                dve.wait_ge(Z["chain"], count[0])

            def rsqrt(cols, n, chain_link, to=32):
                v, y, t = st[:, cols:cols + n], st[:, to:to + n], st[:, 48:48 + n]
                chain_link(dve.tensor_scalar(t.bitcast(i32), v.bitcast(i32), 1, None, ALU.logical_shift_right))
                chain_link(dve.tensor_scalar(y.bitcast(i32), t.bitcast(i32), -1.0, 1597463007.0, ALU.mult, ALU.add))
                chain_link(dve.tensor_scalar(v, v, -0.5, None, ALU.mult))
                for _ in range(4):
                    chain_link(dve.tensor_tensor(t, y, y, ALU.mult))
                    chain_link(dve.tensor_tensor(t, t, v, ALU.mult))
                    chain_link(dve.scalar_tensor_tensor(out=y, in0=t, scalar=1.5, in1=y, op0=ALU.add, op1=ALU.mult))

            def mod_vectors():
                dve.wait_ge(Z["lvec"], 16)
                dve.wait_ge(Z["ada_tr"], 24)
                bias = lvec[:, 0:48].unsqueeze(2).to_broadcast([128, 48, 2])
                dve.tensor_tensor(mod, ps[:, 7, 0:96].rearrange("p (c g) -> p c g", g=2), bias, ALU.add).then_inc(Z["mod"], 1)
                dve.wait_ge(Z["mod"], 1)
                for v, c0 in ((0, 8), (1, 32)):
                    nrm = lvec[:, 48 + 8 * v:56 + 8 * v].unsqueeze(2).to_broadcast([128, 8, 2])
                    dve.scalar_tensor_tensor(out=fold[:, v, :, :], in0=mod[:, c0:c0 + 8, :], scalar=1.0, in1=nrm,
                                             op0=ALU.add, op1=ALU.mult).then_inc(Z["mod"], 1)
                dve.tensor_scalar(fold[:, 2, :, :], mod[:, 16:24, :], 0.5, None, ALU.mult).then_inc(Z["mod"], 1)
                dve.wait_ge(Z["mod"], 4)

            def dense(g):
                s, nt, T = g.s, g.nt, g.T

                def mean(cols, n, width):
                    link(dve.tensor_scalar(st[:, cols:cols + n], st[:, cols:cols + n], 1.0 / width, EPS, ALU.mult, ALU.add))

                dve.wait_ge(s["ss1"], nt)
                mean(0, nt, D)
                rsqrt(0, nt, link)
                for j in range(nt):
                    dve.tensor_scalar(xn[:, j, :], x[:, g.t0 + j, :], st[:, 32 + j:33 + j], None, ALU.mult).then_inc(s["xn"], 1)
                dve.wait_ge(s["ss_qkv"], 2 * nt)
                mean(8, nt, QR)
                mean(8 + nt, nt, KVR)
                rsqrt(8, 2 * nt, link)
                dve.wait_ge(Z["lrow"], 64)
                dve.wait_ge(setup, 16 * 7)
                k0 = g.nk - nt
                for j in range(nt):
                    dve.scalar_tensor_tensor(out=cqn[:, j, :], in0=cqraw[:, j, :], scalar=st[:, 32 + j:33 + j], in1=qn_row[:, :],
                                             op0=ALU.mult, op1=ALU.mult)
                    dve.scalar_tensor_tensor(out=ckvn[:, k0 + j, :], in0=kvraw[:, j, 0:KVR], scalar=st[:, 32 + nt + j:33 + nt + j],
                                             in1=kvn_row[:, :], op0=ALU.mult, op1=ALU.mult)
                    kr = kvraw[:, j, KVR:KVR + ROPE]
                    dst = krp[:, k0 + j, NOPE:HQ]
                    if g.latent:
                        c, sn = trig[:, 0, j, :], trig[:, 1, j, :]
                        ta, tb = rope_tmp[:, 64 * j:64 * j + 32], rope_tmp[:, 64 * j + 32:64 * j + 64]
                        dve.tensor_tensor(ta, kr, c, ALU.mult)
                        dve.tensor_tensor(tb[:, 0:16], kr[:, 16:32], sn[:, 0:16], ALU.mult)
                        link(dve.tensor_tensor(tb[:, 16:32], kr[:, 0:16], sn[:, 16:32], ALU.mult))
                        dve.tensor_tensor(dst, ta, tb, ALU.add).then_inc(s["cn"], 1)
                    else:
                        dve.tensor_copy(dst, kr).then_inc(s["cn"], 1)

                def q_to_heads(i):
                    j, v = i // 2, i % 2
                    dve.wait_ge(s["trq"], i + 1)
                    dve.tensor_copy(qT[0:HQ, 4 * v:4 * v + 4, j * 128:j * 128 + 128],
                                    ps[0:HQ, 4 + i % 4, :].rearrange("p (h t) -> p h t", h=4)).then_inc(s["qT"], 1)

                for j in range(nt):
                    if g.latent:
                        dve.wait_ge(s["q_tm"], j + 1)
                        dve.wait_ge(*((s["q_rope"], j) if j else (s["cn"], nt)))
                        qv = q_tm[:, j % 2, :].rearrange("p (h c) -> p h c", c=HQ)
                        c, sn = (trig[:, v:v + 1, j, :].to_broadcast([128, NH, ROPE]) for v in (0, 1))
                        ta, tb = (rope_tmp[:, v * 256:v * 256 + 256].rearrange("p (h c) -> p h c", h=NH) for v in (0, 1))
                        dve.tensor_tensor(ta, qv[:, :, NOPE:HQ], c, ALU.mult)
                        dve.tensor_tensor(tb[:, :, 0:16], qv[:, :, NOPE + 16:HQ], sn[:, :, 0:16], ALU.mult)
                        link(dve.tensor_tensor(tb[:, :, 16:32], qv[:, :, NOPE:NOPE + 16], sn[:, :, 16:32], ALU.mult))
                        dve.tensor_tensor(qv[:, :, NOPE:HQ], ta, tb, ALU.add).then_inc(s["q_rope"], 1)
                    if j >= 1:
                        q_to_heads(2 * j - 2)
                        q_to_heads(2 * j - 1)
                q_to_heads(2 * nt - 2)
                q_to_heads(2 * nt - 1)
                if g.latent:
                    dve.wait_ge(Z["sc_saved"], 16)
                for i, (h0, nh, kt, n_kt) in enumerate(g.k_pieces):
                    dve.wait_ge(s["k_ps"], i + 1)
                    w = nh * n_kt * 128
                    dve.tensor_copy(KTv(g)[0:NOPE, h0:h0 + nh, kt * 128:(kt + n_kt) * 128],
                                    ps[0:NOPE, i % 4, 0:w].rearrange("p (h t) -> p h t", h=nh)).then_inc(s["kT"], 1)

                def normalise(j):
                    dve.wait_ge(s["o_ps"], NH * (j + 1))
                    link(dve.reciprocal(ssum[:, 32 + 8 * (j % 2):40 + 8 * (j % 2)], ssum[:, NH * j:NH * j + NH]))
                    den = ssum[:, 32 + 8 * (j % 2):40 + 8 * (j % 2)].unsqueeze(2).to_broadcast([128, NH, VD])
                    dve.tensor_tensor(attn_all[:, j, :].rearrange("p (h c) -> p h c", h=NH),
                                      ps[:, 6 + j % 2, :].rearrange("p (h c) -> p h c", h=NH), den, ALU.mult).then_inc(s["attn"], 1)

                for i in range(nt * NH):
                    dve.wait_ge(s["s_ps"], i + 1)
                    if i >= 4:
                        dve.wait_ge(s["prob"], i - 3)
                    b = 2 * (i % 2)
                    dve.tensor_reduce(nmax[:, i % 4:i % 4 + 1], psf[:, b * 512:b * 512 + g.TK], AX.X, ALU.max, negate=True).then_inc(s["smax"], 1)
                    if i >= NH + 3 and (i - 3) % NH == 0:
                        normalise((i - 3) // NH - 1)
                normalise(nt - 1)
                dve.wait_ge(Z["lrow"], 64)
                def sine_argument(i):
                    dve.wait_ge(s["f_ps"], i + 1)
                    if i:
                        dve.wait_ge(s["f"], 1)
                    fa, fn, fr = (ftmp[0:HID, v, 0:T] for v in range(3))
                    link(dve.tensor_scalar(fa, ps[0:HID, i, 0:T], fb[:, i:i + 1], None, ALU.add))
                    link(dve.tensor_scalar(fn, fa, 1.0 / (2 * math.pi), MAGIC, ALU.mult, ALU.add))
                    link(dve.tensor_scalar(fn, fn, -MAGIC, None, ALU.add))
                    link(dve.scalar_tensor_tensor(out=fr, in0=fn, scalar=-TWO_PI_HI, in1=fa, op0=ALU.mult, op1=ALU.add))
                    link(dve.scalar_tensor_tensor(out=fr, in0=fn, scalar=-TWO_PI_LO, in1=fr, op0=ALU.mult, op1=ALU.add))
                    dve.tensor_scalar(fr, fr, 3.1415925, -3.1415925, ALU.min, ALU.max).then_inc(s["f_red"], 1)

                def windowed(o, part):
                    for i in part:
                        i += o * 2 * nt
                        dve.wait_ge(s["h_ps"], i + 1)
                        dve.wait_ge(s["win"], i + 1)
                        if i >= 4:
                            dve.wait_ge(s["sd"], i // 2 - 1)
                        dve.tensor_tensor(wh[:, i % 4, :], ps[:, i % 4, :], win[:, i % 2, :], ALU.mult).then_inc(s["wh"], 1)

                dve.wait_ge(Z["lfil"], 64)
                for m in range(12):
                    b = 4 + m % 4
                    dve.wait_ge(s["hyc_mid"], m + 1)
                    link(dve.scalar_tensor_tensor(out=hyT[:, m, 1:T], in0=ps[:, b, 0:T - 1], scalar=convw[:, m, 0:1], in1=hyT[:, m, 1:T],
                                                  op0=ALU.mult, op1=ALU.add))
                    dve.scalar_tensor_tensor(out=hyT[:, m, 0:T - 1], in0=ps[:, b, 1:T], scalar=convw[:, m, 2:3], in1=hyT[:, m, 0:T - 1],
                                             op0=ALU.mult, op1=ALU.add).then_inc(s["hyc"], 1)
                    if m in (1, 3):
                        sine_argument(m // 2)
                    if m >= 5 and m % 2:
                        windowed(0, beside(g, m // 2))
                for o in (0, 1):
                    if o:
                        windowed(1, range(2 * nt))
                    for kc in range(nt):
                        i = o * nt + kc
                        dve.wait_ge(s["U_ps"], i + 1)
                        dve.wait_ge(s["K"], (o + 1) * 2 * nt)
                        if kc >= 2:
                            dve.wait_ge(s["Yc"], i - 1)
                        b = 4 + 2 * (kc % 2)
                        for v, (ur, kr) in enumerate(((0, 0), (1, 1), (0, 1), (1, 0))):
                            m = dve.tensor_tensor(prodm[:, kc % 2, v, :], ps[:, b + ur, :], Kf[:, kr, kc, :], ALU.mult)
                        m.then_inc(s["Ym"], 1)
                    for c in range(4):
                        dve.wait_ge(s["y_ps"], 4 * o + c + 1)
                        dst = hyT[:, c, 0:T] if o == 0 else hyoT[:, c, 0:T]
                        dve.scalar_tensor_tensor(out=dst, in0=ps[:, c, 0:T], scalar=1.0 / T, in1=hyT[:, 4 * (o + 1) + c, 0:T],
                                                 op0=ALU.mult, op1=ALU.mult).then_inc(s["y"], 1)
                ident3 = ident[:, :].unsqueeze(1).to_broadcast([128, 8, 128])
                vectors = (fold[:, 2, :, g.gi], fold[:, 1, :, g.gi], mod[:, 24:32, g.gi], mod[:, 40:48, g.gi])

                def diagonals(r):
                    if r:
                        dve.wait_ge(s["row_ps"], 2 * r)
                    dve.tensor_tensor(dgr, ident3, vectors[r].unsqueeze(2).to_broadcast([128, 8, 128]), ALU.mult).then_inc(s["dgr"], 1)

                diagonals(0)
                pieces = route(0, scores_back, routing_p)
                for c in range(KD):
                    for v in (0, 1):
                        dve.wait_ge(s["th"], 2 * c + v + 1)
                        dve.wait_ge(s["mg_ps"], 4 * c + 3 + v)
                        if c >= 2:
                            dve.wait_ge(s["mg"], c - 1)
                        m = dve.scalar_tensor_tensor(out=mtmp[:, 2 * (c % 2) + v, 0:T], in0=tg[:, 2 * (c % 2) + v, 0:T], scalar=1.0,
                                                     in1=ps[:, 4 * (c % 2) + 2 + v, 0:T], op0=ALU.add, op1=ALU.mult)
                    m.then_inc(s["mm"], 1)
                    if c < 3:
                        diagonals(c + 1)
                    if g.latent and c >= 3:
                        if c == 3:
                            dve.wait_ge(s["row_ps"], 8)
                            dve.wait_ge(Z["sc_back"], 16)
                        for _ in range(2 if c < 6 else 1):
                            next(pieces, None)
                dve.wait_ge(s["row"], 8)
                def second_norm(j):
                    dve.wait_ge(s["ss2"], j + 1)
                    mean(j, 1, D)
                    rsqrt(j, 1, link, 32 + j)
                    link(dve.scalar_tensor_tensor(out=xn2[:, j, :], in0=x[:, g.t0 + j, :], scalar=st[:, 32 + j:33 + j], in1=rows[:, 1, :],
                                                  op0=ALU.mult, op1=ALU.mult))
                    dve.tensor_tensor(h2_of(g, j), xn2[:, j, :], rows[:, 2, :], ALU.add).then_inc(s["h2"], 1)

                for q in range(4 * nt):
                    i = q % 4
                    dve.wait_ge(s["out_ps"], q + 1)
                    if q >= 2:
                        dve.wait_ge(s["xadd"], q - 1)
                    dve.tensor_tensor(otmp[:, q % 2, :], ps[:, q % 8, 0:256], rows[:, 0, i * 256:i * 256 + 256], ALU.mult).then_inc(s["r2"], 1)
                    if i == 1 and q > 4:
                        second_norm(q // 4 - 1)
                second_norm(nt - 1)
                for i in range(NHP):
                    dve.wait_ge(s["sc_ps"], i + 1)
                    dst = scores[:, :, i, :] if g.latent else scores_p[:, i:i + 1, :]
                    dve.tensor_copy(dst, ps[:, 6 + i % 2, 0:T].rearrange("p (j n) -> p j n", j=nt)).then_inc(s["sc"], 1)
                dve.wait_ge(s["sc"], NHP)

            def step(instrs):
                link(instrs[-1])

            def route(t, sc, v):
                s = of_group
                scr, s16, i16, i16f, expert, cand, cidx, scr2, eq, top, pos, posf, gex, gsum = (v[n] for n in (
                    "scr", "s16", "i16", "i16f", "expert", "cand", "cidx", "scr2", "eq", "top", "pos", "posf", "gex", "gsum"))
                step([dve.max(s16[:, h, 0:8], sc[:, h, :]) for h in range(NHP)])
                step([dve.match_replace(scr[:, h, :], s16[:, h, 0:8], sc[:, h, :], -3.0e38) for h in range(NHP)])
                yield
                step([dve.max(s16[:, h, 8:16], scr[:, h, :]) for h in range(NHP)])
                i16u = i16.bitcast(u32)
                for h in range(NHP):
                    dve.max_index(i16u[:, h, 0:8], s16[:, h, 0:8], sc[:, h, :])
                yield
                step([dve.max_index(i16u[:, h, 8:16], s16[:, h, 8:16], scr[:, h, :]) for h in range(NHP)])
                link(dve.tensor_copy(i16f, i16u))
                v4 = i16f.rearrange("p (h v) k -> p h v k", v=2)
                link(dve.tensor_scalar(v4[:, :, 0, :], v4[:, :, 0, :], float(NK), None, ALU.mult))
                w4 = s16.rearrange("p (h v) k -> p h v k", v=2)
                at = 0
                for i0, n, w in RUNS:
                    for src, dst in ((w4, cand), (v4, cidx)):
                        out = dst[:, :, at:at + n * w].rearrange("p h (n w) -> p h n w", w=w)
                        m = dve.tensor_tensor(out, src[:, :, 0, i0:i0 + n].unsqueeze(3).to_broadcast([128, PH, n, w]),
                                              src[:, :, 1, 0:w].unsqueeze(2).to_broadcast([128, PH, n, w]), ALU.add)
                    at += n * w
                link(m)
                yield
                step([dve.max(top[:, h, 0:8], cand[:, h, :]) for h in range(PH)])
                step([dve.match_replace(scr2[:, h, :], top[:, h, 0:8], cand[:, h, :], -3.0e38) for h in range(PH)])
                step([dve.max(top[:, h, 8:16], scr2[:, h, :]) for h in range(PH)])
                if t:
                    dve.wait_ge(s["gw"], t)
                dve.tensor_tensor(gex, top, top[:, :, 0:1].to_broadcast([128, PH, 16]), ALU.subtract).then_inc(s["top"], 1)
                yield
                posu = pos.bitcast(u32)
                for h in range(PH):
                    dve.max_index(posu[:, h, 0:8], top[:, h, 0:8], cand[:, h, :])
                step([dve.max_index(posu[:, h, 8:16], top[:, h, 8:16], scr2[:, h, :]) for h in range(PH)])
                link(dve.tensor_copy(posf, posu))
                full = [128, 16, NC]
                for h0 in (0, PH // 2):
                    for h in range(PH // 2):
                        m = dve.tensor_tensor(eq[:, h], posf[:, h0 + h, :].unsqueeze(2).to_broadcast(full), iota[:, :].unsqueeze(1).to_broadcast(full), ALU.is_equal)
                    link(m)
                    if h0 == 0:
                        yield
                    for h in range(PH // 2):
                        m = dve.tensor_tensor(eq[:, h], eq[:, h], cidx[:, h0 + h, :].unsqueeze(1).to_broadcast(full), ALU.mult)
                    link(m)
                    if h0:
                        yield
                    link(dve.tensor_reduce(expert[:, h0:h0 + PH // 2, :], eq, AX.X, ALU.add))
                    if h0 == 0:
                        yield
                dve.tensor_scalar(idx[:, t * SLOTS:(t + 1) * SLOTS].rearrange("p (h k) -> p h k", h=PH), expert, loff[:, 0:1], None, ALU.add)
                dve.wait_ge(s["ge"], t + 1)
                link(dve.tensor_reduce(gsum, gex, AX.X, ALU.add))
                link(dve.reciprocal(gsum, gsum))
                link(dve.tensor_scalar(gsum, gsum, 0.5, None, ALU.mult))
                dve.tensor_tensor(gwt[:, t * SLOTS:(t + 1) * SLOTS].rearrange("p (h k) -> p h k", h=PH), gex,
                                  gsum.unsqueeze(2).to_broadcast([128, PH, 16]), ALU.mult).then_inc(s["gw"], 1)

            def half(n, hf, h2, l, between=None):
                m = n * 2 + hf
                q = hf * HALF
                for b in range(HALF):
                    dve.wait_ge(gath[q + b], (l * (TILES * ITERS) + n + 1) * 16)
                    dve.tensor_tensor_reduce(gbuf[q + b][:, 0:D], gbuf[q + b][:, 0:D], h2, 1.0, 0.0, ALU.mult, ALU.add,
                                             dots[:, q + b:q + b + 1]).then_inc(Z["ttr"], 1)
                dv, sq, inn, th, w = (v[:, q:q + HALF] for v in (dots, dsq, din, dth, dw))
                dve.wait_ge(Z["ttr"], m * HALF + HALF)
                dve.tensor_tensor(sq, dv, dv, ALU.mult).then_inc(Z["p_small"], 1)
                dve.wait_ge(Z["p_small"], m * 3 + 1)
                dve.tensor_scalar(sq, sq, GELU_A, 1.0, ALU.mult, ALU.add).then_inc(Z["p_small"], 1)
                dve.wait_ge(Z["p_small"], m * 3 + 2)
                dve.tensor_tensor(inn, sq, dv, ALU.mult).then_inc(Z["inner"], 1)
                dve.wait_ge(Z["th_e"], m + 1)
                dve.scalar_tensor_tensor(out=w, in0=th, scalar=1.0, in1=dv, op0=ALU.add, op1=ALU.mult).then_inc(Z["p_small"], 1)
                dve.wait_ge(Z["p_small"], m * 3 + 3)
                gates = gwt[:, n * NB + q:n * NB + q + HALF] if between is not None else gwt[:, bass.ds(n * NB + q, HALF)]
                dve.tensor_tensor(w, w, gates, ALU.mult).then_inc(Z["w_ready"], 1)
                if between is not None:
                    next(between, None)

            def add_experts(g, t):
                dve.wait_ge(Z["buf_free"], NB + SLOTS * (t + 1))
                dve.tensor_tensor(eacc, ps[:, 0:2, :].rearrange("p b n -> p (b n)"), g2[:, g.gi, :], ALU.mult).then_inc(Z["acc_read"], 1)
                dve.wait_ge(Z["acc_read"], t + 2)
                xt = xflat[:, bass.ds(t * D, D)] if g.latent else xflat[:, 0:D]
                dve.tensor_tensor(xt, xt, eacc, ALU.add).then_inc(Z["pchain"], 1)
                dve.wait_ge(Z["pchain"], t + 1)

            def experts_beside_routing(l):
                for j in range(4):
                    pieces = route(j + 1, scores[:, j], routing_s)
                    for i in range(8):
                        half(4 * j + i // 2, i % 2, h2p[:, :], l, pieces)
                    next(pieces, None)
                add_experts(GR[0], 0)

            def experts(g, l):
                with dve.Fori(1, TILES) as t:
                    dve.tensor_copy(h2c, keep[:, bass.ds((t - 1) * D, D)]).then_inc(Z["h2c"], 1)
                    with dve.Fori(0, ITERS) as i:
                        dve.wait_ge(Z["h2c"], t)
                        for hf in (0, 1):
                            half(t * ITERS + i, hf, h2c, l)
                    add_experts(g, t)

            dve.memset(krp, 0.0).then_inc(silu, 1)
            dve.memset(ones[:, :], 1.0)
            dve.memset(zeros[:, :], 0.0)
            dve.wait_ge(silu, 2)
            dve.scalar_tensor_tensor(out=cth[:, :], in0=cth[:, :], scalar=1.0, in1=cfm[:, :], op0=ALU.add, op1=ALU.mult).then_inc(silu, 1)
            dve.wait_ge(silu, 3)
            dve.tensor_scalar(cfm[:, :], cth[:, :], 0.5, None, ALU.mult).then_inc(silu, 1)
            with dve.Fori(0, DEPTH) as l:
                count[0] = 0
                mod_vectors()
                for g in GR:
                    if g.latent:
                        meet(dve, 2 * l + 1)
                    dense(g)
                dve.tensor_copy(zeros[:, :], zeros[:, :]).then_inc(Z["acc_read"], 1)
                experts_beside_routing(l)
                dve.wait_ge(of_group["gw"], TILES)
                experts(GR[1], l)
                meet(dve, 2 * l + 2)
            fc = [0]

            def flink(ins):
                fc[0] += 1
                ins.then_inc(silu, 1)
                dve.wait_ge(silu, 4 + fc[0])
            dve.wait_ge(final, 16)
            dve.wait_ge(final_sq, TILES)
            flink(dve.tensor_scalar(st[:, 0:TILES], st[:, 0:TILES], 1.0 / D, EPS, ALU.mult, ALU.add))
            rsqrt(0, TILES, flink)
            for j in range(TILES):
                m = dve.scalar_tensor_tensor(out=x[:, j, :], in0=x[:, j, :], scalar=st[:, 32 + j:33 + j], in1=arena[:, 0:D],
                                             op0=ALU.mult, op1=ALU.mult)
            m.then_inc(fch, 1)

        @block.gpsimd
        def _(pool):
            def dense(g):
                s, nt, T = g.s, g.nt, g.T
                done = [0]
                for o in (0, 1):
                    pool.wait_ge(Z["lfil"], 64)
                    for tc in range(nt):
                        i = o * nt + tc
                        pool.wait_ge(s["wh"], 2 * i + 2)
                        if o and tc == 0:
                            pool.wait_ge(s["y_ps"], 4)
                        wf, wb = wh[:, (2 * i) % 4, :], wh[:, (2 * i + 1) % 4, :]
                        if tc == 0:
                            pool.tensor_tensor(Yf[:, 0, tc, :], wf, wb, ALU.add).then_inc(s["bias0"], 1)
                            pool.wait_ge(s["bias0"], o + 1)
                            pool.tensor_tensor(Yf[0:1, 0, 0, :], Yf[0:1, 0, 0, :], hyb[:, o * HYW:(o + 1) * HYW], ALU.add)
                        else:
                            pool.tensor_tensor(Yf[:, 0, tc, :], wf, wb, ALU.add)
                        pool.tensor_tensor(Yf[:, 1, tc, :], wf, wb, ALU.subtract).then_inc(s["sd"], 1)
                    for kc in range(nt):
                        i = o * nt + kc
                        pool.wait_ge(s["Ym"], i + 1)
                        pool.wait_ge(s["K_ps"], (o + 1) * 2 * nt)
                        pr = prodm[:, kc % 2]
                        pool.tensor_tensor(Yf[:, 0, kc, :], pr[:, 0, :], pr[:, 1, :], ALU.subtract)
                        pool.tensor_tensor(Yf[:, 1, kc, :], pr[:, 2, :], pr[:, 3, :], ALU.add).then_inc(s["Yc"], 1)
                for c in range(KD):
                    pool.wait_ge(s["mm"], c + 1)
                    mv = mtmp[:, 2 * (c % 2):2 * (c % 2) + 2, 0:T]
                    pool.tensor_tensor(mergedT[:, c, 0:T], mv[:, 0, :], mv[:, 1, :], ALU.add).then_inc(s["mg"], 1)
                for q in range(4 * nt):
                    i, j = q % 4, q // 4
                    pool.wait_ge(s["r2"], q + 1)
                    xv = x[:, g.t0 + j, i * 256:i * 256 + 256]
                    pool.tensor_tensor(xv, xv, otmp[:, q % 2, :], ALU.add).then_inc(s["xadd"], 1)

            def experts(g):
                def tile(t):
                    with pool.Fori(0, ITERS) as i:
                        for hf in (0, 1):
                            n = t * ITERS + i
                            m = n * 2 + hf
                            q = hf * HALF
                            pool.wait_ge(Z["buf_free"], HALF * m + 1)
                            pool.tensor_copy(estage[:, q:q + HALF], idx[:, bass.ds(n * NB + q, HALF)]).then_inc(Z["staged"], 1)
                            pool.wait_ge(Z["staged"], m + 1)
                            pool.sem_inc(Z["turn"])
                            for b in range(HALF):
                                if b:
                                    pool.wait_ge(Z["buf_free"], HALF * m + b + 1)
                                    pool.sem_inc(Z["turn"])
                                nc.gpsimd.indirect_dma_start(
                                    out=gbuf[q + b], out_offset=None, in_=I["peer_uv"],
                                    in_offset=bass.IndirectOffsetOnAxis(ap=estage[:, q + b:q + b + 1], axis=0)).then_inc(gath[q + b], 16)
                if g.latent:
                    with pool.Fori(1, TILES) as t:
                        tile(t)
                else:
                    tile(0)

            with pool.Fori(0, DEPTH) as l:
                for g in GR:
                    if g.latent:
                        meet(pool, 2 * l + 1)
                    dense(g)
                pool.wait_ge(GR[1].s["sc_ps"], NHP)
                pool.wait_ge(of_group["gw"], 1)
                pool.sem_inc(Z["buf_free"], NB)
                experts(GR[0])
                pool.wait_ge(of_group["gw"], TILES)
                experts(GR[1])
                meet(pool, 2 * l + 2)


def constants():
    f = np.float32
    t = np.arange(DEC_SEQ, dtype=f)
    n_freq = ROPE // 4
    inv = (1.0 / (10000.0 ** (np.arange(n_freq, dtype=f) / n_freq))).astype(f)
    ang = np.concatenate([(t // GRID_W)[:, None] * inv, (t % GRID_W)[:, None] * inv], axis=1).astype(f)
    cos, sin = np.cos(ang), np.sin(ang)
    tab = np.stack([np.concatenate([cos, cos], 1), np.concatenate([-sin, sin], 1)])
    out = {"trig": tab.reshape(2, 4, 128, ROPE).transpose(2, 0, 1, 3).reshape(128, -1)}
    zs, nts = [], []
    for n in (SEQ, DEC_SEQ):
        tt = (np.arange(n, dtype=f) / f(n)).astype(f)
        a = (f(2.0 * math.pi) * tt[:, None] * np.arange(1, BANDS + 1, dtype=f)).astype(f)
        zs.append(np.concatenate([tt[:, None], np.sin(a), np.cos(a)], axis=1).T)
        nts.append(-tt.reshape(-1, 128).T)
    out["zT"] = np.concatenate(zs, axis=1)
    out["negt"] = np.concatenate(nts, axis=1)
    out["ident"] = np.eye(128)
    out["iota"] = np.tile(np.arange(NC), (128, 1))
    out["loff"] = np.stack([np.full((128, 1), l * N_EXPERTS) for l in range(DEPTH)])
    for name, n in (("dft_p", SEQ), ("dft_s", DEC_SEQ)):
        k, tt = np.arange(n)[None, :], np.arange(n)[:, None]
        w = np.pi * (2 * k + 1) / (2 * n)
        mats = [np.cos(w * tt), np.sin(w * tt), np.cos(w * (tt + 0.5)), np.sin(w * (tt + 0.5))]
        out[name] = np.stack(mats).reshape(4, n // 128, 128, n).transpose(0, 2, 1, 3)
    return {k: np.ascontiguousarray(v, dtype=f) for k, v in out.items()}


def packed(w, m):
    l, r, c = w.shape
    return w.reshape(l, r // 128, 128, c // m, m).transpose(0, 3, 2, 1, 4).reshape(l, c // m, 128, r // 128 * m)


def kernel(**inputs):
    from concourse import bacc
    from concourse.bass_utils import run_bass_kernel_spmd

    v = {k: np.asarray(a) for k, a in inputs.items()}
    fm = lambda a: a.reshape(DEPTH, -1, 128).transpose(0, 2, 1)
    arr = {
        "x": np.concatenate([v["x_prompt"][0], v["x_sample"][0]], axis=0),
        "cond": np.stack([v["c_ctx"], v["c"][0]]).reshape(2, KD, 128).transpose(2, 1, 0).reshape(128, 16),
        "w_ada": packed(v["w_ada"], 256), "w_qkv": packed(v["w_in"][:, :, :HY0], HY0), "w_hy": packed(v["w_in"][:, :, HY0:GT0], 256),
        "w_ga": packed(v["w_in"][:, :, GT0:GT0 + D], 256), "w_gb": packed(v["w_in"][:, :, GT0 + D:], 256),
        "w_uq": packed(v["w_uq"], 768), "w_ukv": packed(v["w_ukv"], 1024), "w_out": packed(v["w_out"], 256),
        "w_oab": packed(np.concatenate([v["w_oa"], v["w_ob"]], axis=1), 256), "w_wq": packed(v["peer_wq"], 256),
        "keysT": v["peer_keys"].reshape(DEPTH, NHP, NK, 128).transpose(0, 3, 1, 2).reshape(DEPTH, 128, NHP * NK),
        "lvec": np.concatenate([fm(v["b_ada"]), fm(v["norm_mix"]), fm(v["norm_ffn"])], axis=2),
        "q_norm": v["q_norm"], "kv_norm": v["kv_norm"],
        "cache_ckv": v["cache_ckv"][0], "cache_kr": v["cache_krope"][0],
        "convw": np.concatenate([v["hy_conv_w"], v["hy_conv_b"][:, None]], axis=1).reshape(DEPTH, 4, 12, 128)
            .transpose(0, 3, 2, 1).reshape(DEPTH, 128, 48),
        "hy_w1": v["hy_w1"], "hy_w2": v["hy_w2"], "hy_b": np.stack([v["hy_b1"], v["hy_b2"]], axis=2), "hy_w3": v["hy_w3"],
        "decay": v["hy_decay"].reshape(2 * DEPTH, 2 * HYW),
        "hy_bias": v["hy_bias"].reshape(DEPTH, 1, 2 * HYW),
        "peer_uv": np.concatenate([v["peer_u"], v["peer_v"]], axis=2).reshape(DEPTH * N_EXPERTS, 2 * D),
        "final_norm": v["final_norm"],
    }
    arr.update(constants())
    arr = {"in_" + k: np.ascontiguousarray(a) for k, a in arr.items()}
    nc = bacc.Bacc("TRN2", target_bir_lowering=False, num_devices=1)
    I = {k[3:]: nc.dram_tensor(k, a.shape, mybir.dt.from_np(a.dtype), kind="ExternalInput").ap()
         for k, a in arr.items()}
    O = {k: nc.dram_tensor("out_" + k, s, mybir.dt.float32, kind="ExternalOutput").ap()
                           for k, s in (("y", (SEQ + DEC_SEQ, D)), ("ckv", (DEPTH, 128, KVR)), ("kr", (DEPTH, 128, ROPE)))}
    build(nc, I, O)
    r = run_bass_kernel_spmd(nc, [arr], core_ids=[0]).results[0]
    y = r["out_y"]
    return (y[:SEQ].reshape(1, SEQ, D), y[SEQ:].reshape(1, DEC_SEQ, D),
            r["out_ckv"].reshape(1, DEPTH, SEQ, KVR), r["out_kr"].reshape(1, DEPTH, SEQ, ROPE))
```
